# Optimizing a Trainium2 kernel written in Bass

```python
import math
import jax
import jax.numpy as jnp
from jax import lax
import numpy as np

D_MODEL = 1024
BATCH = 1
SEQ = 256
DEPTH = 1
DEC_BATCH = 1
DEC_SEQ = 1024
PAST_LEN = 128

HEAD_DIM = 64
A_HEADS = 8
A_KV_HEADS = 2
A_GROUP = A_HEADS // A_KV_HEADS
B_HEADS = 8
B_KV_HEADS = 2
B_GROUP = B_HEADS // B_KV_HEADS
A_WIDTH = A_HEADS * HEAD_DIM
B_WIDTH = B_HEADS * HEAD_DIM
KV_A_WIDTH = A_KV_HEADS * HEAD_DIM
KV_B_WIDTH = B_KV_HEADS * HEAD_DIM
Q_BLOCK = 128
WINDOW = 128
GRID_W = 64
ROPE_THETA = 10000.0
AXIS_DIM = HEAD_DIM // 2
N_BUCKETS = 32
MAX_DISTANCE = 128
N_EXPERTS = 16
CAPACITY_FACTOR = 2
D_FF = 2048
N_MOD = 6
EPS = 1e-6
NEG_INF = -1e30

SPLIT_POINTS = (
    A_WIDTH,
    A_WIDTH + KV_A_WIDTH,
    A_WIDTH + 2 * KV_A_WIDTH,
    A_WIDTH + 2 * KV_A_WIDTH + B_WIDTH,
    A_WIDTH + 2 * KV_A_WIDTH + B_WIDTH + KV_B_WIDTH,
    A_WIDTH + 2 * KV_A_WIDTH + B_WIDTH + 2 * KV_B_WIDTH,
    A_WIDTH + 2 * KV_A_WIDTH + B_WIDTH + 2 * KV_B_WIDTH + D_MODEL,
)
IN_COLS = A_WIDTH + 2 * KV_A_WIDTH + B_WIDTH + 2 * KV_B_WIDTH + 2 * D_MODEL

kernel_name = "hybrid_bidir_encoder_ec_moe"

def rms_norm(x, g):
    xf = x.astype(jnp.float32)
    y = xf * lax.rsqrt(jnp.mean(xf * xf, axis=-1, keepdims=True) + EPS)
    return (y * g.astype(jnp.float32)).astype(x.dtype)

def axial_angles(n_tokens):
    rows = n_tokens // GRID_W
    row_pos = jnp.repeat(jnp.arange(rows, dtype=jnp.float32), GRID_W)
    col_pos = jnp.tile(jnp.arange(GRID_W, dtype=jnp.float32), rows)
    inv_freq = ROPE_THETA ** (-jnp.arange(0, AXIS_DIM, 2, dtype=jnp.float32) / AXIS_DIM)
    return row_pos[:, None] * inv_freq, col_pos[:, None] * inv_freq

def rotate_axis(x, ang):
    xf = x.astype(jnp.float32)
    x1, x2 = jnp.split(xf, 2, axis=-1)
    cos = jnp.cos(ang)[None, :, None, :]
    sin = jnp.sin(ang)[None, :, None, :]
    return jnp.concatenate([x1 * cos - x2 * sin, x2 * cos + x1 * sin], axis=-1).astype(x.dtype)

def axial_rope(x, ang_r, ang_c):
    return jnp.concatenate([rotate_axis(x[..., :AXIS_DIM], ang_r),
                            rotate_axis(x[..., AXIS_DIM:], ang_c)], axis=-1)

def t5_bucket(rel):
    half = N_BUCKETS // 2
    max_exact = half // 2
    base = (rel > 0).astype(jnp.int32) * half
    n = jnp.abs(rel)
    large = max_exact + (jnp.log(jnp.maximum(n, 1).astype(jnp.float32) / max_exact)
                         / math.log(MAX_DISTANCE / max_exact) * (half - max_exact)).astype(jnp.int32)
    large = jnp.minimum(large, half - 1)
    return base + jnp.where(n < max_exact, n, large)

def global_attention(q, k, v):
    b, s = q.shape[0], q.shape[1]
    nb = s // Q_BLOCK
    qb = q.reshape(b, nb, Q_BLOCK, A_KV_HEADS, A_GROUP, HEAD_DIM).transpose(1, 0, 2, 3, 4, 5)

    def one_block(qi):
        logits = jnp.einsum('bqkgd,bskd->bkgqs', qi, k, preferred_element_type=jnp.float32)
        p = jax.nn.softmax(logits, axis=-1)
        return jnp.einsum('bkgqs,bskd->bqkgd', p.astype(v.dtype), v)

    o = lax.map(one_block, qb)
    return o.transpose(1, 0, 2, 3, 4, 5).reshape(b, s, A_WIDTH)

def window_attention(q, k, v, rel_bias, sink):
    b, s = q.shape[0], q.shape[1]
    nb = s // Q_BLOCK
    nside = WINDOW // Q_BLOCK
    span = Q_BLOCK + 2 * WINDOW
    pad = ((0, 0), (WINDOW, WINDOW), (0, 0), (0, 0))
    kblk = jnp.pad(k, pad).reshape(b, nb + 2 * nside, Q_BLOCK, B_KV_HEADS, HEAD_DIM)
    vblk = jnp.pad(v, pad).reshape(b, nb + 2 * nside, Q_BLOCK, B_KV_HEADS, HEAD_DIM)
    kw = jnp.concatenate([kblk[:, j:j + nb] for j in range(2 * nside + 1)], axis=2)
    vw = jnp.concatenate([vblk[:, j:j + nb] for j in range(2 * nside + 1)], axis=2)
    qb = q.reshape(b, nb, Q_BLOCK, B_KV_HEADS, B_GROUP, HEAD_DIM)
    logits = jnp.einsum('bnqkgd,bnskd->bnkgqs', qb, kw, preferred_element_type=jnp.float32)

    qpos = jnp.arange(Q_BLOCK)
    spos = jnp.arange(span)
    rel = spos[None, :] - WINDOW - qpos[:, None]
    band = jnp.abs(rel) <= WINDOW
    kabs = jnp.arange(nb)[:, None] * Q_BLOCK - WINDOW + spos[None, :]
    inside = (kabs >= 0) & (kabs < s)
    mask = band[None, :, :] & inside[:, None, :]
    bias = rel_bias.astype(jnp.float32)[t5_bucket(rel)]
    bias = bias.transpose(2, 0, 1).reshape(B_KV_HEADS, B_GROUP, Q_BLOCK, span)
    logits = jnp.where(mask[None, :, None, None], logits + bias, NEG_INF)

    sink_l = sink.astype(jnp.float32).reshape(B_KV_HEADS, B_GROUP)[:, :, None, None]
    m = jnp.maximum(jnp.max(logits, axis=-1, keepdims=True), sink_l)
    p = jnp.exp(logits - m)
    p = p / (jnp.sum(p, axis=-1, keepdims=True) + jnp.exp(sink_l - m))
    o = jnp.einsum('bnkgqs,bnskd->bnqkgd', p.astype(v.dtype), vw)
    return o.reshape(b, s, B_WIDTH)

def expert_choice_moe(h, w_router, w_e_gate, w_e_up, w_e_down):
    b, s, d = h.shape
    n = b * s
    cap = CAPACITY_FACTOR * n // N_EXPERTS
    t = h.reshape(n, d)
    aff = jax.nn.softmax(jnp.einsum('nd,de->ne', t, w_router, preferred_element_type=jnp.float32), axis=-1)
    g, idx = lax.top_k(aff.T, cap)
    xe = t[idx]
    hid = jax.nn.silu(jnp.einsum('ecd,edf->ecf', xe, w_e_gate)) * jnp.einsum('ecd,edf->ecf', xe, w_e_up)
    ye = jnp.einsum('ecf,efd->ecd', hid, w_e_down) * g[..., None].astype(h.dtype)
    out = jnp.zeros((n, d), ye.dtype).at[idx.reshape(-1)].add(ye.reshape(-1, d))
    return out.reshape(b, s, d)

def encoder_layer(x, c, ang_r, ang_c, w_ada, b_ada, norm1_g, w_in, q_norm_g, k_norm_g, sink,
                  w_branch_a, w_branch_b, w_out, norm2_g, w_router, w_e_gate, w_e_up, w_e_down, rel_bias):
    b, s = x.shape[0], x.shape[1]
    mod = (jax.nn.silu(c) @ w_ada + b_ada)[:, None, :]
    sh1, sc1, gt1, sh2, sc2, gt2 = jnp.split(mod, N_MOD, axis=-1)

    h = rms_norm(x, norm1_g) * (1 + sc1) + sh1
    qa, ka, va, qb, kb, vb, ga, gb = jnp.split(h @ w_in, SPLIT_POINTS, axis=-1)

    qa = axial_rope(rms_norm(qa.reshape(b, s, A_HEADS, HEAD_DIM), q_norm_g), ang_r, ang_c) * (HEAD_DIM ** -0.5)
    ka = axial_rope(rms_norm(ka.reshape(b, s, A_KV_HEADS, HEAD_DIM), k_norm_g), ang_r, ang_c)
    oa = global_attention(qa, ka, va.reshape(b, s, A_KV_HEADS, HEAD_DIM)) @ w_branch_a

    ob = window_attention(qb.reshape(b, s, B_HEADS, HEAD_DIM) * (HEAD_DIM ** -0.5),
                          kb.reshape(b, s, B_KV_HEADS, HEAD_DIM),
                          vb.reshape(b, s, B_KV_HEADS, HEAD_DIM), rel_bias, sink) @ w_branch_b

    merged = jax.nn.sigmoid(ga) * oa + jax.nn.sigmoid(gb) * ob
    x = x + gt1 * (merged @ w_out)

    h2 = rms_norm(x, norm2_g) * (1 + sc2) + sh2
    x = x + gt2 * expert_choice_moe(h2, w_router, w_e_gate, w_e_up, w_e_down)
    return x

def setup_inputs(seed: int = 0) -> dict:
    key = jax.random.key(seed)
    ks = jax.random.split(key, 24)

    def nrm(k, shape, scale):
        return jax.random.normal(k, shape, jnp.float32) * scale

    def gain(k, shape):
        return 1.0 + 0.02 * jax.random.normal(k, shape, jnp.float32)

    return {
        "x_prompt": nrm(ks[0], (BATCH, SEQ, D_MODEL), 1.0),
        "x_sample": nrm(ks[1], (DEC_BATCH, DEC_SEQ, D_MODEL), 1.0),
        "c_prompt": nrm(ks[2], (BATCH, D_MODEL), 1.0),
        "c_sample": nrm(ks[3], (DEC_BATCH, D_MODEL), 1.0),
        "w_ada": nrm(ks[4], (DEPTH, D_MODEL, N_MOD * D_MODEL), 0.5 * D_MODEL ** -0.5),
        "b_ada": nrm(ks[5], (DEPTH, N_MOD * D_MODEL), 0.01),
        "norm1_g": gain(ks[6], (DEPTH, D_MODEL)),
        "w_in": nrm(ks[7], (DEPTH, D_MODEL, IN_COLS), D_MODEL ** -0.5),
        "q_norm_g": gain(ks[8], (DEPTH, HEAD_DIM)),
        "k_norm_g": gain(ks[9], (DEPTH, HEAD_DIM)),
        "sink": nrm(ks[10], (DEPTH, B_HEADS), 0.5),
        "w_branch_a": nrm(ks[11], (DEPTH, A_WIDTH, D_MODEL), A_WIDTH ** -0.5),
        "w_branch_b": nrm(ks[12], (DEPTH, B_WIDTH, D_MODEL), B_WIDTH ** -0.5),
        "w_out": nrm(ks[13], (DEPTH, D_MODEL, D_MODEL), D_MODEL ** -0.5),
        "norm2_g": gain(ks[14], (DEPTH, D_MODEL)),
        "w_router": nrm(ks[15], (DEPTH, D_MODEL, N_EXPERTS), D_MODEL ** -0.5),
        "w_e_gate": nrm(ks[16], (DEPTH, N_EXPERTS, D_MODEL, D_FF), D_MODEL ** -0.5),
        "w_e_up": nrm(ks[17], (DEPTH, N_EXPERTS, D_MODEL, D_FF), D_MODEL ** -0.5),
        "w_e_down": nrm(ks[18], (DEPTH, N_EXPERTS, D_FF, D_MODEL), D_FF ** -0.5),
        "rel_bias": nrm(ks[19], (N_BUCKETS, B_HEADS), 0.5),
        "norm_f_g": gain(ks[20], (D_MODEL,)),
    }

def reference(x_prompt, x_sample, c_prompt, c_sample, w_ada, b_ada, norm1_g, w_in, q_norm_g, k_norm_g,
              sink, w_branch_a, w_branch_b, w_out, norm2_g, w_router, w_e_gate, w_e_up, w_e_down,
              rel_bias, norm_f_g):
    def trunk(x, c):
        ang_r, ang_c = axial_angles(x.shape[1])
        for l in range(DEPTH):
            x = encoder_layer(x, c, ang_r, ang_c, w_ada[l], b_ada[l], norm1_g[l], w_in[l], q_norm_g[l],
                              k_norm_g[l], sink[l], w_branch_a[l], w_branch_b[l], w_out[l], norm2_g[l],
                              w_router[l], w_e_gate[l], w_e_up[l], w_e_down[l], rel_bias)
        return rms_norm(x, norm_f_g)

    y_prompt = trunk(x_prompt, c_prompt)
    y_sample = trunk(x_sample, c_sample)
    return (y_prompt, y_sample)


_drawn_inputs = setup_inputs


def setup_inputs(seed=0):
    import zlib

    import numpy as np

    out = dict(_drawn_inputs(seed))
    spreads = {}
    factors = {'b_ada': 8.0,
     'norm1_g': 8.0,
     'q_norm_g': 8.0,
     'k_norm_g': 8.0,
     'sink': 8.0,
     'norm2_g': 8.0,
     'rel_bias': 5.213,
     'norm_f_g': 2.952}
    for name, (base, spread) in spreads.items():
        noise = np.random.default_rng([zlib.crc32(name.encode()), seed]).standard_normal(out[name].shape)
        drawn = base * np.exp(spread * noise) if base else spread * noise
        out[name] = jnp.asarray(drawn.astype(out[name].dtype))
    for name, factor in factors.items():
        out[name] = (out[name] * factor).astype(out[name].dtype)
    return out
```

```python
from contextlib import ExitStack

import numpy as np

import concourse.bass as bass
from concourse import mybir

F32 = mybir.dt.float32
U32 = mybir.dt.uint32
ALU = mybir.AluOpType
ACT = mybir.ActivationFunctionType
AX = mybir.AxisListType

P = 128
D = 1024
KD = D // P
SEQ, DEC = 256, 1024
TOK = SEQ + DEC
NT = TOK // P
PT_TILES = SEQ // P
HD = 64
NPAIR = 4
QKV = 1536
WIN = 128
N_BUCKETS, MAX_DISTANCE = 32, 128
GRID_W, THETA = 64, 10000.0
NE = 16
CAP_S, CAP_P = 2 * DEC // NE, 2 * SEQ // NE
SLOTS = CAP_S + CAP_P
FF = 2048
KF = FF // P
EPS = 1e-6
NEG = -1e30
RELW = 511
CH = 4096


def rope_tables():
    t = np.arange(DEC)
    inv = (THETA ** (-np.arange(0, 32, 2, dtype=np.float32) / np.float32(32))).astype(np.float32)
    row = (t // GRID_W).astype(np.float32)[:, None] * inv
    col = (t % GRID_W).astype(np.float32)[:, None] * inv
    c = np.concatenate([np.cos(row), np.cos(row), np.cos(col), np.cos(col)], 1).astype(np.float32)
    s = np.concatenate([-np.sin(row), np.sin(row), -np.sin(col), np.sin(col)], 1).astype(np.float32)
    return tuple(np.ascontiguousarray(x.reshape(8, P, HD).transpose(1, 0, 2)) for x in (c, s))


def bucket_onehot():
    rel = np.arange(RELW) - 255
    half = N_BUCKETS // 2
    exact = half // 2
    n = np.abs(rel)
    large = exact + (np.log(np.maximum(n, 1).astype(np.float32) / np.float32(exact))
                     / np.float32(np.log(MAX_DISTANCE / exact)) * np.float32(half - exact)).astype(np.int32)
    b = (rel > 0) * half + np.where(n < exact, n, np.minimum(large, half - 1))
    m = np.zeros((33, RELW), np.float32)
    m[b, np.arange(RELW)] = 1.0
    m[:, n > WIN] = 0.0
    m[32, n > WIN] = 1.0
    return m


def group_of(t):
    return 0 if t < PT_TILES else 1


def attention_items():
    items = []
    for br in (0, 1):
        for lo, hi in ((0, PT_TILES), (PT_TILES, NT)):
            for qt in range(lo, hi):
                kts = list(range(lo, hi)) if br == 0 else list(range(max(lo, qt - 1), min(hi, qt + 2)))
                items += [(br, j, qt, kts) for j in range(NPAIR)]
    return items


def plan_steps(items):
    s = [("vec",)] + [("br", h) for h in range(8)]
    s += [("XP", 0), ("XP", 1), ("AR", 0), ("AR", 1), ("AC", 0), ("AR", 2), ("AC", 1), ("AR", 3), ("AC", 2),
          ("AC", 3), ("A1",), ("X", 0), ("XP", 2), ("X", 1), ("tab",)]
    for t in range(NT):
        s.append(("G", t))
        if t + 2 < NT:
            s.append(("X", t + 2))
        if t >= 1:
            s.append(("Q", t - 1))
        s.append(("N", t))
        if t + 3 < NT:
            s.append(("XP", t + 3))
    s.append(("Q", NT - 1))
    c = 4
    for i in range(len(items)):
        s.append(("S", i))
        if i >= 1:
            s += [("T", i - 1), ("R", i), ("PV", i - 1)]
        else:
            s.append(("R", i))
        if i >= 12 and i % 5 == 0 and c < 12:
            s += [("AR", c), ("AC", c)]
            c += 1
    s += [("T", len(items) - 1), ("PV", len(items) - 1), ("A2",)]
    s += [("GT", n) for n in range(4)]
    s += [("M", m, n) for m in range(KD) for n in range(3)]
    for t in range(NT + 3):
        if t < NT:
            s.append(("O", t))
        if 0 <= t - 1 < NT:
            s.append(("X2", t - 1))
        if 0 <= t - 2 < NT:
            s.append(("RT", t - 2))
        if 0 <= t - 3 < NT:
            s.append(("AT", t - 3))
        if t == 6:
            s.append(("K", 0))
        if t < NT:
            s.append(("XO", t))
    s += [("GT", n) for n in range(4, 8)]
    s += [("K", 1), ("I",)]
    return s


def t_jobs(step, items):
    k = step[0]
    if k in ("X", "X2"):
        return [(step, 0), (step, 1)]
    if k == "Q":
        return [(step, n) for n in range(3)]
    if k in ("vec", "br", "AR", "AC", "GT", "AT"):
        return [(step, 0)]
    if k == "T":
        return [(step, (hh, a)) for hh in range(2) for a in range(0, len(items[step[1]][3]), 4)]
    if k == "I":
        return [(step, n) for n in range(4)]
    return []


def encoder(nc, x_p, x_s, c_p, c_s, w_ada, b_ada, n1g, w_in, qg, kg, sink, w_ba, w_bb, w_out, n2g, w_router,
            w_gate, w_up, w_down, rel_bias, nfg, rope_c, rope_s, onehot, y_p, y_s):
    items = attention_items()
    NI = len(items)
    steps = plan_steps(items)
    jobs = [j for s in steps for j in t_jobs(s, items)]
    job_at = {j: n for n, j in enumerate(jobs)}

    x_d = [x_p[0], x_s[0]]
    y_d = [y_p[0], y_s[0]]
    ada_v = w_ada[0].rearrange("(k p) n -> p k n", p=P)
    win_v = w_in[0].rearrange("(k p) n -> p k n", p=P)
    wout_v = w_out[0].rearrange("(k p) n -> p k n", p=P)
    wbr_v = [w[0].rearrange("(v j p) n -> v p j n", v=2, j=NPAIR) for w in (w_ba, w_bb)]

    acc_d = [nc.dram_tensor("acc_prompt", [SEQ, D], F32).ap(), nc.dram_tensor("acc_sample", [DEC, D], F32).ap()]
    xn_d = [nc.dram_tensor("xn_prompt", [SEQ, D], F32).ap(), nc.dram_tensor("xn_sample", [DEC, D], F32).ap()]
    brow_d = nc.dram_tensor("bias_rows", [P * 8 * RELW + 8], F32)

    def token_rows(d, t):
        g = group_of(t)
        r = (t - (PT_TILES if g else 0)) * P
        return d[g][r:r + P, :]

    with ExitStack() as ctx:
        def sb(name, shape, dt=F32):
            return ctx.enter_context(nc.sbuf_tensor(name, shape, dt))

        def sem(name):
            return ctx.enter_context(nc.semaphore(name))

        arena = sb("arena", [P, 50688])

        def at(o, *dims):
            n = int(np.prod(dims))
            v = arena[:, o:o + n]
            if len(dims) == 2:
                v = v.rearrange("p (a b) -> p a b", a=dims[0])
            if len(dims) == 3:
                v = v.rearrange("p (a b c) -> p a b c", a=dims[0], b=dims[1])
            if len(dims) == 4:
                v = v.rearrange("p (a b c d) -> p a b c d", a=dims[0], b=dims[1], c=dims[2])
            return v

        hT = at(0, KD, TOK)
        qT = at(10240, 2, NPAIR, TOK)
        kz = at(20480, 2, 2, TOK)
        V = at(25600, 2, NT, P)
        R3, R4 = 28160, 40448
        ada_slot = {c: o for c, o in enumerate([0, 4096, 10240, 14336])}
        ada_slot.update({c: R3 + CH * ((c - 4) % 3) for c in range(4, 12)})
        wqkv = [at(R3 + CH * c, KD, 512) for c in range(3)]
        brow = at(20480, 8, RELW)
        relb = at(26700, 8, P)[0:33]
        oneh = at(24600, RELW)[0:33]
        modrow0 = at(R4, 2, 512)
        xt = at(R4, 2, D)
        xn = at(R4 + 2048, 2, D)
        raw = at(R4 + 4096, QKV)
        rawB = raw[:, 768:1280].rearrange("p (j v d) -> p j v d", j=NPAIR, v=2)
        sq = at(R4 + 5632, 10, HD)
        t2 = at(R4 + 6272, 10, HD)
        qf = at(R4 + 6912, 2, 10, HD)
        tabs = at(R4 + 8192, 4, 8, HD)
        modrow0 = at(R4 + 6912, 2, 512)
        Pb = at(R4, 2, 2, 1024)
        PT = at(R4 + 4096, 2, 8, P)
        biasm = at(R4 + 6144, 8, 384)
        modrow1 = at(R4 + 9216, 2, 512)
        dg = at(R4, 2, 4, P)
        merged = at(R3, KD, TOK)
        mw = [20480, 20480 + 3072]
        wo = [at(38400, KD, 512), at(38400 + CH, KD, 512)]
        sig = at(46592, 2, 2, 512)
        gt1b = at(48640, 2, D)
        xo = at(20480, 2, D)
        x1 = at(22528, 2, D)
        xn2 = at(24576, 2, D)
        h2T = [at(26624, KD, P), at(46592, KD, P)]
        affS = at(47616, DEC)[0:NE]
        ring = [0, 4096, 8192, 12288, 16384, R3]
        B = R3 + CH
        hidT = at(B, KF, SLOTS)
        xeT = at(B + 2560, KD, SLOTS)
        yeT = at(B + 3840, KD, SLOTS)
        xeS, xeP = at(B + 5120, D), at(B + 6144, D)[0:CAP_P]
        yeS, yeP = at(B + 7168, D), at(B + 8192, D)[0:CAP_P]
        gt2b = at(B + 9216, 2, D)
        sil = at(B + 11264, 2, SLOTS)
        nfb = at(B + 12288, D)
        fin = at(0, NT, D)
        finy = at(10240, NT, D)

        ident = sb("ident", [P, P])
        ones = sb("ones", [P, P])
        vec = sb("vec", [80, P])
        spare = sb("spare", [P, 1])
        vecT = sb("vecT", [P, 80])
        modT = sb("modT", [P, 48, 2])
        A1 = sb("A1", [P, KD, 2])
        A2 = sb("A2", [P, KD, 2])
        cS = sb("cS", [P, KD, 32])
        sel = sb("sel", [P, 2])
        wr = sb("wr", [P, KD, NE])
        gains = sb("gains", [P, 2, HD])
        snk = sb("snk", [P, 8])
        nsnk = sb("nsnk", [P, 8])
        relc = sb("relc", [32, 8])
        st = sb("st", [P, 2, 2, 8])
        rs = sb("rs", [P, 2, 8])
        qs = sb("qs", [P, 5, 10])
        affP = sb("affP", [NE, SEQ])
        lg = sb("lg", [P, 2, NE])
        af = sb("af", [P, 2, NE])
        rst = sb("rst", [P, 2, 4])
        top = [sb("top_p", [NE, CAP_P]), sb("top_s", [NE, CAP_S])]
        ti = [sb("ti_p", [NE, CAP_P], U32), sb("ti_s", [NE, CAP_S], U32)]
        tif = [sb("tif_p", [NE, CAP_P]), sb("tif_s", [NE, CAP_S])]
        idx = [sb("idx_p", [CAP_P, NE + 1], U32), sb("idx_s", [CAP_S, NE + 1], U32)]
        gv = [sb("gv_p", [CAP_P, NE]), sb("gv_s", [CAP_S, NE])]
        gidx = [sb("gidx_p", [CAP_P, 1], U32), sb("gidx_s", [CAP_S, 1], U32)]
        sidx = [sb("sidx_p", [CAP_P, 1], U32), sb("sidx_s", [CAP_S, 1], U32)]
        ps = ctx.enter_context(nc.psum_tensor("ps", [P, 8, 512], F32))

        small_in, table_in = sem("small_in"), sem("table_in")
        ada_in = [sem(f"ada_in{n}") for n in range(7)]
        win_in = sem("win_in")
        x_in = [sem(f"x_in{n}") for n in range(2)]
        bias_out, bias_in = sem("bias_out"), sem("bias_in")
        const = sem("const")
        relb_ready = sem("relb_ready")
        kz_zero = sem("kz_zero")
        t_done = sem("t_done")
        t_free = [sem(f"t_free{n}") for n in range(3)]
        cs_ready, vec_ready = sem("cs_ready"), sem("vec_ready")
        modrow_ready, mod_ready = sem("modrow_ready"), sem("mod_ready")
        a1_ready = sem("a1_ready")
        brow_ready = sem("brow_ready")
        chain = sem("chain")
        ssq = sem("ssq")
        rms_in, rms_sqrt = sem("rms_in"), sem("rms_sqrt")
        xn_ready = sem("xn_ready")
        hT_ready = sem("hT_ready")
        g_done, g_free, raw_ready = sem("g_done"), [sem(f"g_free{n}") for n in range(5)], sem("raw_ready")
        q_in, q_sqrt, qf_ready, tab_ready = sem("q_in"), sem("q_sqrt"), sem("qf_ready"), sem("tab_ready")
        qT_ready, kz_ready = sem("qT_ready"), sem("kz_ready")
        s_done, nm_ready, e_done, es_done = sem("s_done"), sem("nm_ready"), sem("e_done"), sem("es_done")
        b_done = sem("b_done")
        rinv_ready, pn_ready = sem("rinv_ready"), sem("pn_ready")
        pt_v, pt_a = sem("pt_v"), sem("pt_a")
        pv_done, o_done = sem("pv_done"), sem("o_done")
        a2_ready, dg_ready, gt_ready = sem("a2_ready"), sem("dg_ready"), sem("gt_ready")
        mw_in, wo_in = [sem("mw_in0"), sem("mw_in1")], [sem("wo_in0"), sem("wo_in1")]
        m_done, sig_ready, mm_ready, merged_ready = sem("m_done"), sem("sig_ready"), sem("mm_ready"), sem("merged_ready")
        out_done, out_free = sem("out_done"), sem("out_free")
        xo_in = [sem("xo_in0"), sem("xo_in1")]
        x1_ready, xn2_ready = sem("x1_ready"), sem("xn2_ready")
        x1_out, xn2_out = [sem("x1_out0"), sem("x1_out1")], [sem("xn2_out0"), sem("xn2_out1")]
        h2_ready, r_done, rmax, rexp, aff_ready, affT_ready = (sem("h2_ready"), sem("r_done"), sem("rmax"), sem("rexp"),
                                                               sem("aff_ready"), sem("affT_ready"))
        topk_ready, idx_ready = sem("topk_ready"), sem("idx_ready")
        w_ld = [sem(f"w_ld{n}") for n in range(6)]
        nf_in = sem("nf_in")
        cidx = sem("cidx")
        gat = [sem("gat_p"), sem("gat_s")]
        sca = [sem("sca_p"), sem("sca_s")]
        xe_done, xe_ready = sem("xe_done"), sem("xe_ready")
        gu_done, sil_done, hid_done = sem("gu_done"), sem("sil_done"), sem("hid_done")
        dn_done, yT_done = sem("dn_done"), sem("yT_done")
        yt_done, ye_done, gated = sem("yt_done"), sem("ye_done"), sem("gated")
        experts_done = sem("experts_done")
        f_in = [sem(f"f_in{n}") for n in range(NT)]
        f_ss, f_v, f_sq, y_ready, y_out = sem("f_ss"), sem("f_v"), sem("f_sq"), sem("y_ready"), sem("y_out")

        def bank_of(n):
            return 5 + n % 3

        order = {s: n for n, s in enumerate(steps)}
        before = lambda kind, s: sum(1 for x in steps[:order[s]] if x[0] == kind)
        n_exp = lambda i, hh: 2 * i + hh + 1
        n_add = lambda i, hh: 2 * sum(1 for x in items[:i] if x[0] == 1) + hh + 1
        last_v_pt = [sum(-(-len(x[3]) // 4) for x in items[:i + 1]) for i in range(NI)]

        block = ctx.enter_context(nc.Block())

        @block.sync
        def _(sp):
            rows = [(0, 8, c_p[0].rearrange("(r p) -> r p", p=P)), (8, 8, c_s[0].rearrange("(r p) -> r p", p=P)),
                    (16, 48, b_ada[0].rearrange("(r p) -> r p", p=P)),
                    (64, 8, n1g[0].rearrange("(r p) -> r p", p=P)), (72, 8, n2g[0].rearrange("(r p) -> r p", p=P))]
            for r, n, src in rows:
                sp.dma_start(vec[r:r + n, :], src).then_inc(small_in, 16)
            sp.dma_start(relc[:], rel_bias).then_inc(small_in, 16)
            sp.dma_start(oneh, onehot).then_inc(small_in, 16)
            for t in range(2):
                sp.dma_start(xt[:, t], token_rows(x_d, t)).then_inc(x_in[t], 16)
            for c in range(4):
                sp.dma_start(at(ada_slot[c], KD, 512), ada_v[:, :, c * 512:(c + 1) * 512]).then_inc(ada_in[c], 16)
            sp.dma_start(gains[:, 0], qg[0].partition_broadcast(P)).then_inc(table_in, 16)
            sp.dma_start(gains[:, 1], kg[0].partition_broadcast(P)).then_inc(table_in, 16)
            sp.dma_start(snk[:], sink[0].partition_broadcast(P)).then_inc(table_in, 16)
            sp.dma_start(tabs[:, 0], rope_c).then_inc(table_in, 16)
            sp.dma_start(tabs[:, 1], rope_s).then_inc(table_in, 16)
            sp.dma_start(tabs[:, 2], rope_c).then_inc(table_in, 16)
            sp.dma_start(tabs[:, 3], rope_s).then_inc(table_in, 16)
            for k in range(3):
                a, b = [(0, 3), (3, 6), (6, 8)][k]
                sp.dma_start(wr[:, a:b, :], w_router[0].rearrange("(k p) e -> p k e", p=P)[:, a:b, :])\
                    .then_inc(table_in, 16)
            for c in range(3):
                sp.dma_start(wqkv[c], win_v[:, :, c * 512:(c + 1) * 512]).then_inc(win_in, 16)
            sp.wait_ge(brow_ready, 8)
            sp.dma_start(brow_d.ap()[0:P * 8 * RELW].rearrange("(p n) -> p n", p=P),
                         brow.rearrange("p h r -> p (h r)")).then_inc(bias_out, 16)
            for t in range(2, NT):
                sp.wait_ge(xn_ready, t - 1)
                sp.dma_start(xt[:, t % 2], token_rows(x_d, t)).then_inc(x_in[t % 2], 16)
            sp.wait_ge(g_done, 3 * NT)
            for c in range(4, 7):
                sp.dma_start(at(ada_slot[c], KD, 512), ada_v[:, :, c * 512:(c + 1) * 512]).then_inc(ada_in[4 + (c - 4) % 3], 16)
            sp.wait_ge(bias_out, 16)
            sp.wait_ge(t_done, job_at[(("Q", NT - 1), 2)] + 1)
            skew = bass.AP(tensor=brow_d, offset=127, ap=[[8 * RELW - 1, P], [RELW, 8], [1, 384]])
            sp.dma_start(biasm, skew).then_inc(bias_in, 16)
            for c in range(7, 12):
                sp.wait_ge(t_done, job_at[(("AR", c - 3), 0)] + 1)
                sp.dma_start(at(ada_slot[c], KD, 512), ada_v[:, :, c * 512:(c + 1) * 512]).then_inc(ada_in[4 + (c - 4) % 3], 16)
            sp.wait_ge(pv_done, NI)
            for m in range(KD):
                if m >= 2:
                    sp.wait_ge(m_done, 3 * (m - 1))
                w = mw[m % 2]
                for b in range(2):
                    c0 = QKV + b * D + m * P
                    sp.dma_start(at(w + 1024 * b, KD, P), win_v[:, :, c0:c0 + P]).then_inc(mw_in[m % 2], 16)
                    for v in range(2):
                        sp.dma_start(at(w + 2048 + 512 * b, NPAIR, P)[v * 64:v * 64 + 64],
                                     wbr_v[b][v][:, :, m * P:(m + 1) * P]).then_inc(mw_in[m % 2], 16)
                if m == 1:
                    sp.wait_ge(gt_ready, 4)
                    for h in range(2):
                        sp.dma_start(wo[h], wout_v[:, :, h * 512:(h + 1) * 512]).then_inc(wo_in[h], 16)
            sp.wait_ge(m_done, 3 * KD)
            sp.wait_ge(mm_ready, 3 * KD)

            def chunk_src(e, c):
                if c < 8:
                    w = (w_gate, w_up)[c % 2]
                    return w[0, e].rearrange("(k p) n -> p k n", p=P)[:, :, (c // 2) * 512:(c // 2 + 1) * 512]
                return w_down[0, e].rearrange("(k p) n -> p k n", p=P)[:, :, (c - 8) * 256:(c - 7) * 256]

            def load_chunk(e, c):
                s = c % 6
                dst = at(ring[s], KD, 512) if c < 8 else at(ring[s], KF, 256)
                sp.dma_start(dst, chunk_src(e, c)).then_inc(w_ld[s], 16)

            for t in range(2):
                sp.dma_start(xo[:, t], token_rows(x_d, t)).then_inc(xo_in[t], 16)
            for t in range(NT):
                if t + 2 < NT:
                    sp.wait_ge(x1_ready, t + 1)
                    sp.dma_start(xo[:, t % 2], token_rows(x_d, t + 2)).then_inc(xo_in[t % 2], 16)
                if t < 5:
                    load_chunk(0, t)
            sp.wait_ge(out_done, NT)
            load_chunk(0, 5)
            sp.wait_ge(gt_ready, 8)
            sp.dma_start(nfb, nfg.partition_broadcast(P)).then_inc(nf_in, 16)
            def used(e, c):
                return (gu_done, 16 * e + 4 * (c // 2) + 4) if c < 8 else (dn_done, 8 * e + 2 * (c - 8) + 2)

            with sp.Fori(0, NE - 1) as e:
                for s in (0, 3, 5):
                    sp.wait_ge(*used(e, s))
                    load_chunk(e, 6 + s)
                    load_chunk(e, 6 + (s ^ 1))
                for s in (0, 2, 3, 4, 5):
                    sp.wait_ge(*used(e, 6 + s))
                    load_chunk(e + 1, s)
                    if s == 0:
                        load_chunk(e + 1, 1)
            for s in range(6):
                sp.wait_ge(*used(NE - 1, s))
                load_chunk(NE - 1, 6 + s)
            sp.wait_ge(dn_done, 8 * NE)
            sp.wait_ge(sca[0], 16 * NE)
            sp.wait_ge(sca[1], 16 * NE)
            for t in range(NT):
                sp.dma_start(fin[:, t], token_rows(acc_d, t)).then_inc(f_in[t], 16)
            for t in range(NT):
                sp.wait_ge(y_ready, t + 1)
                sp.dma_start(token_rows(y_d, t), finy[:, t]).then_inc(y_out, 16)
            sp.wait_ge(y_out, 16 * NT)

        @block.gpsimd
        def _(gp):
            gp.memset(ident[:], 0.0).then_inc(const, 1)
            gp.memset(sel[:], 0.0).then_inc(const, 1)
            gp.memset(ones[:], 1.0).then_inc(const, 1)
            gp.memset(cS[:], 0.0).then_inc(const, 1)
            gp.wait_ge(const, 4)
            gp.affine_select(out=ident[:], in_=ident[:], compare_op=ALU.not_equal, fill=1.0, base=0,
                             pattern=[[-1, P]], channel_multiplier=1).then_inc(const, 1)
            for q in range(4):
                gp.affine_select(out=sel[:], in_=sel[:], compare_op=ALU.not_equal, fill=1.0, base=-32 * q,
                                 pattern=[[-1, 2]], channel_multiplier=1).then_inc(const, 1)
                gp.wait_ge(const, 6 + q)
            for b in range(2):
                gp.memset(idx[b][:, NE:NE + 1], 0).then_inc(const, 1)
            for s in steps:
                k = s[0]
                if k == "G" and s[1] == 0:
                    gp.wait_ge(bias_out, 16)
                    gp.wait_ge(t_done, job_at[(("AC", 3), 0)] + 1)
                    gp.memset(kz, 0.0).then_inc(kz_zero, 1)
                if k == "R":
                    i = s[1]
                    w = len(items[i][3]) * P
                    for hh in range(2):
                        gp.wait_ge(rinv_ready, 2 * i + hh + 1)
                        p_ = Pb[:, i % 2, hh, 0:w]
                        gp.tensor_scalar(p_, p_, st[:, i % 2, hh, 3:4], None, ALU.mult).then_inc(pn_ready, 1)
                if k == "M":
                    n = (s[1] * 3 + s[2])
                    w = 256 if s[2] == 2 else 512
                    gp.wait_ge(mm_ready, n + 1)
                    gp.tensor_tensor(merged[:, s[1], s[2] * 512:s[2] * 512 + w], sig[:, n % 2, 0, 0:w],
                                     sig[:, n % 2, 1, 0:w], ALU.add).then_inc(merged_ready, 1)
                if k in ("XO",):
                    t = s[1]
                    gp.wait_ge(xn2_ready, t + 1)
                    gp.dma_start(token_rows(xn_d, t), xn2[:, t % 2]).then_inc(xn2_out[t % 2], 16)
                    gp.dma_start(token_rows(acc_d, t), x1[:, t % 2]).then_inc(x1_out[t % 2], 16)

            def gather(e_idx):
                for b, dst in ((1, xeS), (0, xeP)):
                    gp.indirect_dma_start(out=dst, out_offset=None, in_=xn_d[b],
                                          in_offset=bass.IndirectOffsetOnAxis(ap=gidx[b][:, 0:1], axis=0))\
                        .then_inc(gat[b], 16)

            def gate(n=None):
                if n is not None:
                    gp.wait_ge(gated, n)
                gp.tensor_tensor(spare[:, 0:1], ones[:, 0:1], ones[:, 1:2], ALU.add).then_inc(gated, 1)

            for b in range(2):
                gp.wait_ge(xn2_out[b], 16 * (NT // 2))
                gp.wait_ge(x1_out[b], 16 * (NT // 2))
            gp.wait_ge(idx_ready, 4)
            for b in range(2):
                gp.tensor_copy(gidx[b][:], idx[b][:, 0:1]).then_inc(cidx, 1)
            gp.wait_ge(cidx, 2)
            gather(0)
            gate()
            with gp.Fori(0, NE) as e:
                for b in range(2):
                    gp.wait_ge(gat[b], 16 * e + 16)
                gp.wait_ge(xe_done, 3 * e + 3)
                gate(4 * e + 1)
                for b in range(2):
                    gp.tensor_copy(gidx[b][:], idx[b][:, bass.ds(e + 1, 1)]).then_inc(cidx, 1)
                    gp.tensor_copy(sidx[b][:], idx[b][:, bass.ds(e, 1)]).then_inc(cidx, 1)
                gp.wait_ge(cidx, 4 * e + 6)
                gate(4 * e + 2)
                gather(e)
                gp.wait_ge(ye_done, 4 * e + 5)
                gate(4 * e + 3)
                for b, src in ((1, yeS), (0, yeP)):
                    gp.indirect_dma_start(out=acc_d[b], out_offset=bass.IndirectOffsetOnAxis(ap=sidx[b][:, 0:1], axis=0),
                                          in_=src, in_offset=None, compute_op=ALU.add).then_inc(sca[b], 16)
                gp.wait_ge(sca[0], 16 * e + 16)
                gp.wait_ge(sca[1], 16 * e + 16)
                gate(4 * e + 4)
            gp.wait_ge(gat[0], 16 * NE + 16)
            gp.wait_ge(gat[1], 16 * NE + 16)

        @block.scalar
        def _(ac):
            def job(s, n=0):
                j = job_at[(s, n)]
                ac.wait_ge(t_done, j + 1)
                return ps[:, bank_of(j)], t_free[j % 3]

            for s in steps:
                k = s[0]
                if k == "vec":
                    b, free = job(s)
                    ac.wait_ge(const, 4)
                    ac.activation(cS[:, :, 0:2].rearrange("p k g -> p g k"),
                                  b[:, 0:16].rearrange("p (g k) -> p g k", g=2), ACT.Silu).then_inc(cs_ready, 1)
                    ac.activation(vecT[:], b[:, 0:80], ACT.Copy).then_inc(free, 1)
                if k == "br":
                    b, free = job(s)
                    ac.activation(brow[:, s[1], :], b[:, 0:RELW], ACT.Copy).then_inc(brow_ready, 1)
                if k == "AR":
                    c = s[1]
                    b, free = job(s)
                    if c >= 2:
                        ac.wait_ge(t_done, job_at[(("AC", c - 2), 0)] + 1)
                    ac.activation((modrow0 if c < 4 else modrow1)[:, c % 2], b, ACT.Copy).then_inc(modrow_ready, 1)
                if k == "XP":
                    t = s[1]
                    ac.wait_ge(x_in[t % 2], 16 * (t // 2 + 1))
                    if t >= 2:
                        ac.wait_ge(t_done, job_at[(("X", t - 2), 1)] + 1)
                    ac.activation(xn[:, t % 2], xt[:, t % 2], ACT.Square, accum_out=rs[:, t % 2, 0:1]).then_inc(ssq, 1)
                    ac.wait_ge(rms_in, t + 1)
                    ac.activation(rs[:, t % 2, 2:3], rs[:, t % 2, 1:2], ACT.Sqrt).then_inc(rms_sqrt, 1)
                if k == "G":
                    t = s[1]
                    if t >= 1:
                        ac.wait_ge(t_done, job_at[(("Q", t - 1), 2)] + 1)
                        ac.wait_ge(qf_ready, t)
                    for c in range(3):
                        ac.wait_ge(g_done, 3 * t + c + 1)
                        n = 3 * t + c
                        b = ps[:, n % 5]
                        if c:
                            v0 = 128 if c == 1 else 384
                            if t == 0:
                                ac.wait_ge(kz_zero, 1)
                            ac.activation(V[:, c - 1, t, :], b[:, v0:v0 + P], ACT.Copy).then_inc(raw_ready, 1)
                        if c == 0:
                            ins = ac.activation(raw[:, 0:512], b, ACT.Copy)
                        elif c == 1:
                            ac.activation(raw[:, 512:640], b[:, 0:P], ACT.Copy)
                            ins = ac.activation(rawB[:, :, 0, :], b[:, 256:512].rearrange("p (j d) -> p j d", j=NPAIR),
                                                ACT.Copy)
                        else:
                            ac.activation(rawB[:, :, 1, :], b[:, 0:256].rearrange("p (j d) -> p j d", j=NPAIR), ACT.Copy)
                            ins = ac.activation(raw[:, 1280:1408], b[:, 256:384], ACT.Copy)
                        ins.then_inc(g_free[n % 5], 1)
                if k == "N":
                    t = s[1]
                    ac.wait_ge(q_in, t + 1)
                    ac.activation(qs[:, 2], qs[:, 1], ACT.Sqrt).then_inc(q_sqrt, 1)
                if k == "Q":
                    t = s[1]
                    for br in range(2):
                        b, free = job(s, br)
                        ac.activation(qT[:, br, :, t * P:(t + 1) * P], b.rearrange("p (j q) -> p j q", j=NPAIR),
                                      ACT.Copy, scale=1.0 if br == 0 else HD ** -0.5).then_inc(free, 1)
                if k == "S":
                    i = s[1]
                    br, j, qt, kts = items[i]
                    w = len(kts) * P
                    for hh in range(2):
                        h = j + 4 * hh
                        ac.wait_ge(nm_ready, 2 * i + hh + 1)
                        p_ = Pb[:, i % 2, hh, 0:w]
                        src = p_ if br else ps[:, 2 * hh:2 * hh + 2].rearrange("p a b -> p (a b)")[:, 0:w]
                        ac.activation(p_, src, ACT.Exp, bias=st[:, i % 2, hh, 0:1],
                                      accum_out=st[:, i % 2, hh, 1:2]).then_inc(e_done, 1)
                        if br:
                            ac.activation(st[:, i % 2, hh, 2:3], snk[:, h:h + 1], ACT.Exp,
                                          bias=st[:, i % 2, hh, 0:1]).then_inc(es_done, 1)
                if k == "T":
                    i = s[1]
                    kts = items[i][3]
                    for a in range(0, len(kts), 4):
                        n = min(4, len(kts) - a)
                        b, free = job(s, (1, a))
                        ac.activation(PT[:, 1, a:a + n, :], b[:, 0:n * P].rearrange("p (n q) -> p n q", n=n),
                                      ACT.Copy).then_inc(free, 1)
                if k == "PV":
                    i = s[1]
                    br, j, qt, kts = items[i]
                    ac.wait_ge(pv_done, i + 1)
                    ac.activation(qT[:, br, j, qt * P:(qt + 1) * P], ps[:, 4, 0:P], ACT.Copy).then_inc(o_done, 1)
                if k == "GT":
                    n = s[1]
                    b, free = job(s)
                    dst = (gt1b, gt2b)[n // 4]
                    ac.activation(dst[:, (n // 2) % 2, (n % 2) * 512:(n % 2) * 512 + 512], b, ACT.Copy)\
                        .then_inc(gt_ready, 1)
                if k == "M":
                    n = s[1] * 3 + s[2]
                    w = 256 if s[2] == 2 else 512
                    ac.wait_ge(m_done, n + 1)
                    if n >= 2:
                        ac.wait_ge(merged_ready, n - 1)
                    for b in range(2):
                        ac.activation(sig[:, n % 2, b, 0:w], ps[:, 4 * (n % 2) + b, 0:w], ACT.Sigmoid)\
                            .then_inc(sig_ready, 1)
                if k == "XO":
                    t = s[1]
                    ac.wait_ge(x1_ready, t + 1)
                    if t >= 2:
                        ac.wait_ge(t_done, job_at[(("X2", t - 2), 1)] + 1)
                        ac.wait_ge(xn2_out[t % 2], 16 * (t // 2))
                    ac.activation(xn2[:, t % 2], x1[:, t % 2], ACT.Square, accum_out=rs[:, t % 2, 0:1]).then_inc(ssq, 1)
                    ac.wait_ge(rms_in, NT + t + 1)
                    ac.activation(rs[:, t % 2, 2:3], rs[:, t % 2, 1:2], ACT.Sqrt).then_inc(rms_sqrt, 1)
                if k == "RT":
                    t = s[1]
                    ac.wait_ge(rmax, t + 1)
                    ac.activation(lg[:, t % 2], ps[:, 4, 0:NE], ACT.Exp, bias=rst[:, t % 2, 0:1],
                                  accum_out=rst[:, t % 2, 1:2]).then_inc(rexp, 1)

            with ac.Fori(0, NE) as e:
                for f in range(KF):
                    ac.wait_ge(gu_done, 16 * e + f + 1)
                    if f >= 2:
                        ac.wait_ge(hid_done, 16 * e + f - 1)
                    ac.activation(sil[:, f % 2], ps[:, f % 3, 0:SLOTS], ACT.Silu).then_inc(sil_done, 1)
                for d in range(KD):
                    ac.wait_ge(dn_done, 8 * e + d + 1)
                    ac.activation(yeT[:, d, :], ps[:, 3 + d % 2, 0:SLOTS], ACT.Copy).then_inc(yT_done, 1)
            for t in range(NT):
                ac.wait_ge(f_in[t], 16)
                ac.activation(finy[:, t], fin[:, t], ACT.Square, accum_out=rs[:, t % 2, 4:5]).then_inc(f_ss, 1)
                ac.wait_ge(f_v, t + 1)
                ac.activation(rs[:, t % 2, 6:7], rs[:, t % 2, 5:6], ACT.Sqrt).then_inc(f_sq, 1)

        @block.vector
        def _(ve):
            count = [0]

            def link(ins):
                count[0] += 1
                ins.then_inc(chain, 1)
                ve.wait_ge(chain, count[0])

            def job(s, n=0):
                j = job_at[(s, n)]
                ve.wait_ge(t_done, j + 1)
                return ps[:, bank_of(j)], t_free[j % 3]

            def mod_affine(A, gain0, m):
                link(ve.tensor_scalar(A[:], modT[:, m:m + KD, :], 1.0, None, ALU.add))
                for g in range(2):
                    link(ve.tensor_tensor(A[:, :, g], A[:, :, g], vecT[:, gain0:gain0 + KD], ALU.mult))

            def norm_in(n):
                ve.wait_ge(ssq, n + 1)
                t = n % NT
                ve.tensor_scalar(rs[:, t % 2, 1:2], rs[:, t % 2, 0:1], 1.0 / D, EPS, ALU.mult, ALU.add).then_inc(rms_in, 1)
                ve.wait_ge(rms_sqrt, n + 1)
                link(ve.reciprocal(rs[:, t % 2, 3:4], rs[:, t % 2, 2:3]))

            def modulate(s, dst, A, sh, g):
                for half in range(2):
                    b, free = job(s, half)
                    for q in range(4):
                        kk = half * 4 + q
                        ins = ve.tensor_scalar(dst(kk), b[:, q * P:(q + 1) * P], A[:, kk, g:g + 1],
                                               modT[:, sh + kk, g:g + 1], ALU.mult, ALU.add)
                    ins.then_inc(free, 1)

            def topk(b, a):
                n = (CAP_P, CAP_S)[b] // 8
                for r in range(n):
                    v = top[b][:, r * 8:r * 8 + 8]
                    link(ve.max(v, a))
                    ve.max_index(ti[b][:, r * 8:r * 8 + 8], v, a)
                    link(ve.match_replace(a, v, a, -1.0))
                ve.tensor_copy(tif[b][:], ti[b][:]).then_inc(topk_ready, 1)

            ve.memset(relb, NEG).then_inc(chain, 1)
            count[0] += 1
            ve.wait_ge(chain, count[0])
            ve.wait_ge(small_in, 16 * 7)
            for h in range(8):
                ins = ve.tensor_copy(relb[0:32, h, :], relc[:, h:h + 1].to_broadcast([32, P]))
            ins.then_inc(relb_ready, 1)
            for s in steps:
                k = s[0]
                if k == "AC":
                    c = s[1]
                    b, free = job(s)
                    if c == 0:
                        ve.wait_ge(t_free[job_at[(("vec",), 0)] % 3], 1)
                    ve.tensor_tensor(modT[:, 4 * c:4 * c + 4, :], b[:, 0:8].rearrange("p (n g) -> p n g", n=4),
                                     vecT[:, 16 + 4 * c:20 + 4 * c].unsqueeze(2).to_broadcast([P, 4, 2]),
                                     ALU.add).then_inc(mod_ready, 1)
                if k == "A1":
                    ve.wait_ge(mod_ready, 4)
                    mod_affine(A1, 64, 8)
                if k == "A2":
                    ve.wait_ge(mod_ready, 12)
                    mod_affine(A2, 72, 32)
                if k == "tab":
                    ve.wait_ge(table_in, 16 * 10)
                    link(ve.tensor_scalar(nsnk[:], snk[:], -1.0, None, ALU.mult))
                    for n in range(2):
                        for x in range(8):
                            tc_, ts_ = tabs[:, 2 * n, x], tabs[:, 2 * n + 1, x]
                            ve.tensor_tensor(tc_, tc_, gains[:, n], ALU.mult)
                            for a in range(2):
                                ins = ve.tensor_tensor(
                                    ts_.rearrange("p (u a v) -> p u a v", u=2, a=2)[:, :, a],
                                    ts_.rearrange("p (u a v) -> p u a v", u=2, a=2)[:, :, a],
                                    gains[:, n].rearrange("p (u a v) -> p u a v", u=2, a=2)[:, :, 1 - a], ALU.mult)
                    link(ins)
                    link(ve.tensor_scalar(tabs[:, 0:2], tabs[:, 0:2], HD ** -0.5, None, ALU.mult))
                if k == "XP":
                    t = s[1]
                    norm_in(t)
                    ve.tensor_scalar(xn[:, t % 2], xt[:, t % 2], rs[:, t % 2, 3:4], None, ALU.mult).then_inc(xn_ready, 1)
                if k == "X":
                    t = s[1]
                    modulate(s, lambda kk: hT[:, kk, t * P:(t + 1) * P], A1, 0, group_of(t))
                if k == "N":
                    t = s[1]
                    for c in range(3):
                        n = 3 * t + c
                        ve.wait_ge(g_free[n % 5], n // 5 + 1)
                    rope_t = (t if t < PT_TILES else t - PT_TILES)
                    r10 = raw[:, 0:640].rearrange("p (h d) -> p h d", h=10)
                    link(ve.tensor_tensor(sq, r10, r10, ALU.mult))
                    link(ve.tensor_reduce(qs[:, 0], sq, AX.X, ALU.add))
                    ve.tensor_scalar(qs[:, 1], qs[:, 0], 1.0 / HD, EPS, ALU.mult, ALU.add).then_inc(q_in, 1)
                    ve.wait_ge(q_sqrt, t + 1)
                    link(ve.reciprocal(qs[:, 3], qs[:, 2]))
                    link(ve.tensor_tensor(qs[:, 4], qs[:, 3], qs[:, 3], ALU.mult))
                    link(ve.tensor_tensor(qs[:, 4], qs[:, 4], qs[:, 1], ALU.mult))
                    link(ve.tensor_scalar(qs[:, 4], qs[:, 4], -0.5, 1.5, ALU.mult, ALU.add))
                    link(ve.tensor_tensor(qs[:, 3], qs[:, 3], qs[:, 4], ALU.mult))
                    link(ve.tensor_tensor(sq, r10, qs[:, 3].unsqueeze(2).to_broadcast([P, 10, HD]), ALU.mult))
                    out = qf[:, t % 2]
                    for n, (a, z) in enumerate(((0, 8), (8, 10))):
                        tc_ = tabs[:, 2 * n, rope_t]
                        ve.tensor_tensor(r10[:, a:z], sq[:, a:z], tc_.unsqueeze(1).to_broadcast([P, z - a, HD]), ALU.mult)
                        for hf in range(2):
                            for u in range(2):
                                o1 = u * 32 + hf * 16
                                o2 = u * 32 + (1 - hf) * 16
                                ins = ve.tensor_tensor(
                                    t2[:, a:z, o1:o1 + 16], sq[:, a:z, o2:o2 + 16],
                                    tabs[:, 2 * n + 1, rope_t, o1:o1 + 16].unsqueeze(1).to_broadcast([P, z - a, 16]),
                                    ALU.mult)
                    link(ins)
                    ve.tensor_tensor(out[:, 0:8].rearrange("p (j v) d -> p v j d", v=2),
                                     r10[:, 0:8].rearrange("p (v j) d -> p v j d", v=2),
                                     t2[:, 0:8].rearrange("p (v j) d -> p v j d", v=2), ALU.add)
                    ve.tensor_tensor(out[:, 8:10], r10[:, 8:10], t2[:, 8:10], ALU.add).then_inc(qf_ready, 1)
                if k == "Q":
                    t = s[1]
                    if t == 0:
                        ve.wait_ge(kz_zero, 1)
                    b, free = job(s, 2)
                    for v in range(2):
                        r = slice(v * 64, v * 64 + 64)
                        ins = ve.tensor_copy(kz[r, :, v, t * P:(t + 1) * P],
                                             b[r, 0:256].rearrange("p (b q) -> p b q", b=2))
                    ins.then_inc(free, 1)
                if k == "S":
                    i = s[1]
                    br, j, qt, kts = items[i]
                    w = len(kts) * P
                    for hh in range(2):
                        h = j + 4 * hh
                        ve.wait_ge(s_done, 2 * i + hh + 1)
                        src = ps[:, 2 * hh:2 * hh + 2].rearrange("p a b -> p (a b)")[:, 0:w]
                        nm = st[:, i % 2, hh, 0:1]
                        if br == 0:
                            ve.tensor_reduce(nm, src, AX.X, ALU.max, negate=True).then_inc(nm_ready, 1)
                        else:
                            ve.wait_ge(bias_in, 16)
                            b0 = (kts[0] - qt + 1) * P
                            p_ = Pb[:, i % 2, hh, 0:w]
                            ve.tensor_tensor(p_, src, biasm[:, h, b0:b0 + w], ALU.add).then_inc(b_done, 1)
                            ve.wait_ge(b_done, n_add(i, hh))
                            link(ve.tensor_reduce(nm, p_, AX.X, ALU.max, negate=True))
                            ve.tensor_tensor(nm, nm, nsnk[:, h:h + 1], ALU.min).then_inc(nm_ready, 1)
                if k == "R":
                    i = s[1]
                    br = items[i][0]
                    for hh in range(2):
                        ve.wait_ge(e_done, 2 * i + hh + 1)
                        f = st[:, i % 2, hh]
                        den = f[:, 1:2]
                        if br:
                            ve.wait_ge(es_done, n_add(i, hh))
                            link(ve.tensor_tensor(den, f[:, 1:2], f[:, 2:3], ALU.add))
                        ve.reciprocal(f[:, 3:4], den).then_inc(rinv_ready, 1)
                if k == "T":
                    i = s[1]
                    kts = items[i][3]
                    for a in range(0, len(kts), 4):
                        n = min(4, len(kts) - a)
                        b, free = job(s, (0, a))
                        ve.tensor_copy(PT[:, 0, a:a + n, :], b[:, 0:n * P].rearrange("p (n q) -> p n q", n=n))\
                            .then_inc(free, 1)
                if k == "GT":
                    n = s[1]
                    if n == 0:
                        ve.wait_ge(o_done, NI)
                    if n % 4 >= 2:
                        ve.wait_ge(t_done, job_at[(("GT", n - 2), 0)] + 1)
                    m0, g = (16, 40)[n // 4], (n // 2) % 2
                    for q in range(4):
                        mm = m0 + (n % 2) * 4 + q
                        ins = ve.tensor_scalar(dg[:, n % 2, q, :], ident[:], modT[:, mm, g:g + 1], None, ALU.mult)
                    ins.then_inc(dg_ready, 1)
                if k == "M":
                    n = s[1] * 3 + s[2]
                    w = 256 if s[2] == 2 else 512
                    for b in range(2):
                        ve.wait_ge(sig_ready, 2 * n + 2)
                        x = sig[:, n % 2, b, 0:w]
                        ins = ve.tensor_tensor(x, x, ps[:, 4 * (n % 2) + 2 + b, 0:w], ALU.mult)
                    ins.then_inc(mm_ready, 1)
                if k == "XO":
                    t = s[1]
                    g = group_of(t)
                    ve.wait_ge(out_done, t + 1)
                    ve.wait_ge(xo_in[t % 2], 16 * (t // 2 + 1))
                    if t >= 2:
                        ve.wait_ge(x1_out[t % 2], 16 * (t // 2))
                    o = ps[:, 2 * (t % 2):2 * (t % 2) + 2].rearrange("p a b -> p (a b)")
                    ve.tensor_tensor(x1[:, t % 2], o, gt1b[:, g], ALU.mult).then_inc(out_free, 1)
                    ve.wait_ge(out_free, t + 1)
                    ve.tensor_tensor(x1[:, t % 2], x1[:, t % 2], xo[:, t % 2], ALU.add).then_inc(x1_ready, 1)
                    norm_in(NT + t)
                    ve.tensor_scalar(xn2[:, t % 2], x1[:, t % 2], rs[:, t % 2, 3:4], None, ALU.mult).then_inc(xn2_ready, 1)
                if k == "X2":
                    t = s[1]
                    modulate(s, lambda kk: h2T[t % 2][:, kk, :], A2, 24, group_of(t))
                if k == "RT":
                    t = s[1]
                    ve.wait_ge(r_done, t + 1)
                    ve.tensor_reduce(rst[:, t % 2, 0:1], ps[:, 4, 0:NE], AX.X, ALU.max, negate=True).then_inc(rmax, 1)
                    ve.wait_ge(rexp, t + 1)
                    link(ve.reciprocal(rst[:, t % 2, 2:3], rst[:, t % 2, 1:2]))
                    ve.tensor_scalar(af[:, t % 2], lg[:, t % 2], rst[:, t % 2, 2:3], None, ALU.mult).then_inc(aff_ready, 1)
                if k == "AT":
                    t = s[1]
                    b, free = job(s)
                    if t < PT_TILES:
                        dst = affP[:, t * P:(t + 1) * P]
                    else:
                        dst = affS[:, (t - PT_TILES) * P:(t - PT_TILES + 1) * P]
                    link(ve.tensor_copy(dst, b[0:NE, 0:P]))
                    ve.engine_nop().then_inc(free, 1)
                if k == "K":
                    topk(s[1], affP[:] if s[1] == 0 else affS)
                if k == "I":
                    for n in range(4):
                        b, free = job(s, n)
                        g, what = n // 2, n % 2
                        c = (CAP_P, CAP_S)[g]
                        dst = gv[g][:] if what else idx[g][:, 0:NE]
                        ve.tensor_copy(dst, b[0:c, 0:NE]).then_inc(idx_ready, 1)

            def xe_evac(wait_n, jobs_done):
                for b3 in range(3):
                    ve.wait_ge(xe_done, jobs_done + b3 + 1)
                    for d in range(3 * b3, min(3 * b3 + 3, KD)):
                        o = (d - 3 * b3) * SLOTS
                        for g, a, z in ((1, 0, CAP_S), (0, CAP_S, SLOTS)):
                            ins = ve.tensor_scalar(xeT[:, d, a:z], ps[:, 5 + b3, o + a:o + z], A2[:, d, g:g + 1],
                                                   modT[:, 24 + d, g:g + 1], ALU.mult, ALU.add)
                    ins.then_inc(xe_ready, 1)

            xe_evac(0, 0)
            ve.memset(rst[:, 0, 0:1], 0.0).then_inc(ye_done, 1)
            with ve.Fori(0, NE) as e:
                for f in range(KF):
                    ve.wait_ge(sil_done, 16 * e + f + 1)
                    ve.tensor_tensor(hidT[:, f, :], sil[:, f % 2], ps[:, f % 3, SLOTS:2 * SLOTS], ALU.mult)\
                        .then_inc(hid_done, 1)
                xe_evac(0, 3 * e + 3)
                ve.wait_ge(gated, 4 * e + 1)
                for n, (g, half, bank) in enumerate(((1, 0, 3), (1, 1, 4), (0, 0, 5), (0, 1, 6))):
                    c = (CAP_P, CAP_S)[g]
                    ve.wait_ge(yt_done, 4 * e + n + 1)
                    ve.scalar_tensor_tensor(out=(yeP, yeS)[g][0:c, half * 512:half * 512 + 512], in0=ps[0:c, bank],
                                            scalar=gv[g][:, bass.ds(e, 1)], in1=gt2b[0:c, g, half * 512:half * 512 + 512],
                                            op0=ALU.mult, op1=ALU.mult).then_inc(ye_done, 1)
            ve.wait_ge(nf_in, 16)
            for t in range(NT):
                ve.wait_ge(f_ss, t + 1)
                ve.tensor_scalar(rs[:, t % 2, 5:6], rs[:, t % 2, 4:5], 1.0 / D, EPS, ALU.mult, ALU.add).then_inc(f_v, 1)
                ve.wait_ge(f_sq, t + 1)
                link(ve.reciprocal(rs[:, t % 2, 7:8], rs[:, t % 2, 6:7]))
                ve.scalar_tensor_tensor(out=finy[:, t], in0=fin[:, t], scalar=rs[:, t % 2, 7:8], in1=nfb,
                                        op0=ALU.mult, op1=ALU.mult).then_inc(y_ready, 1)

        @block.tensor
        def _(pe):
            freed = {}
            uses = [0, 0, 0]
            for n, (s, _) in enumerate(jobs):
                if s[0] == "br":
                    freed[n] = (brow_ready, s[1] + 1)
                elif s[0] == "AR":
                    freed[n] = (modrow_ready, s[1] + 1)
                elif s[0] == "AC":
                    freed[n] = (mod_ready, s[1] + 1)
                elif s[0] == "GT":
                    freed[n] = (gt_ready, s[1] + 1)
                elif s[0] == "I":
                    freed[n] = (idx_ready, jobs[n][1] + 1)
                else:
                    uses[n % 3] += 1
                    freed[n] = (t_free[n % 3], uses[n % 3])

            def bank(s, n=0):
                j = job_at[(s, n)]
                if j >= 3:
                    pe.wait_ge(*freed[j - 3])
                return ps[:, bank_of(j)]

            def drained():
                for q in range(3):
                    pe.wait_ge(*freed[last_job[0] - q])

            last_job = [0]
            for s in steps:
                k = s[0]
                js = t_jobs(s, items)
                if js:
                    last_job[0] = job_at[js[-1]]
                if k == "vec":
                    pe.wait_ge(small_in, 16 * 7)
                    pe.wait_ge(const, 5)
                    b = bank(s)
                    pe.transpose(b[:, 0:80], vec[:], ident[0:80, 0:80]).then_inc(t_done, 1)
                if k == "br":
                    if s[1] == 0:
                        pe.wait_ge(relb_ready, 1)
                    b = bank(s)
                    pe.matmul(b[:, 0:RELW], relb[:, s[1], :], oneh, start=True, stop=True).then_inc(t_done, 1)
                if k == "AR":
                    c = s[1]
                    b = bank(s)
                    if c == 0:
                        pe.wait_ge(cs_ready, 1)
                    pe.wait_ge(ada_in[c] if c < 4 else ada_in[4 + (c - 4) % 3], 16 if c < 4 else 16 * ((c - 4) // 3 + 1))
                    wv = at(ada_slot[c], KD, 512)
                    for kk in range(KD):
                        q = kk % 4
                        ins = pe.matmul(b[32 * q:32 * q + 32, :], cS[:, kk, :], wv[:, kk, :], start=(kk < 4), stop=(kk >= 4),
                                        tile_position=(0, 32 * q))
                    ins.then_inc(t_done, 1)
                if k == "AC":
                    c = s[1]
                    b = bank(s)
                    pe.wait_ge(modrow_ready, c + 1)
                    pe.wait_ge(const, 9)
                    mr = (modrow0 if c < 4 else modrow1)[:, c % 2]
                    for q in range(4):
                        ins = pe.matmul(b[:, 2 * q:2 * q + 2], mr[:, q * P:(q + 1) * P], sel[:], start=(q == 0), stop=True,
                                        skip_group_check=True)
                    ins.then_inc(t_done, 1)
                if k in ("X", "X2"):
                    t = s[1]
                    pe.wait_ge(xn_ready if k == "X" else xn2_ready, t + 1)
                    src = (xn if k == "X" else xn2)[:, t % 2]
                    for half in range(2):
                        b = bank(s, half)
                        for q in range(4):
                            kk = half * 4 + q
                            ins = pe.transpose(b[:, q * P:(q + 1) * P], src[:, kk * P:(kk + 1) * P], ident[:])
                        ins.then_inc(t_done, 1)
                if k == "G":
                    t = s[1]
                    jx = job_at[(("X", t), 1)]
                    pe.wait_ge(*freed[jx])
                    pe.wait_ge(*freed[jx - 1])
                    for c in range(3):
                        n = 3 * t + c
                        if t == 0:
                            pe.wait_ge(win_in, 48)
                        if n >= 5:
                            pe.wait_ge(g_free[n % 5], n // 5)
                        for kk in range(KD):
                            ins = pe.matmul(ps[:, n % 5], hT[:, kk, t * P:(t + 1) * P], wqkv[c][:, kk, :],
                                            start=(kk == 0), stop=(kk == KD - 1))
                        ins.then_inc(g_done, 1)
                if k == "Q":
                    t = s[1]
                    pe.wait_ge(qf_ready, t + 1)
                    f = qf[:, t % 2]
                    b = bank(s, 0)
                    for j in range(NPAIR):
                        ins = pe.transpose(b[:, j * P:(j + 1) * P], f[:, 2 * j:2 * j + 2, :], ident[:])
                    ins.then_inc(t_done, 1)
                    b = bank(s, 1)
                    for j in range(NPAIR):
                        ins = pe.transpose(b[:, j * P:(j + 1) * P], rawB[:, j], ident[:])
                    ins.then_inc(t_done, 1)
                    b = bank(s, 2)
                    pe.transpose(b[:, 0:P], f[:, 8:10, :], ident[:])
                    pe.transpose(b[:, P:2 * P], raw[:, 1280:1408], ident[:]).then_inc(t_done, 1)
                if k == "S":
                    i = s[1]
                    br, j, qt, kts = items[i]
                    k0, w = kts[0] * P, len(kts) * P
                    if i == 0:
                        drained()
                        for n in range(3 * NT - 5, 3 * NT):
                            pe.wait_ge(g_free[n % 5], n // 5 + 1)
                    for hh in range(2):
                        if i >= 1:
                            if items[i - 1][0] == 0:
                                pe.wait_ge(e_done, n_exp(i - 1, hh))
                            else:
                                pe.wait_ge(b_done, n_add(i - 1, hh))
                        for a in range(0, w, 512):
                            z = min(a + 512, w)
                            ins = pe.matmul(ps[:, 2 * hh + a // 512, 0:z - a], qT[:, br, j, qt * P:(qt + 1) * P],
                                            kz[:, br, hh, k0 + a:k0 + z], start=True, stop=True)
                        ins.then_inc(s_done, 1)
                if k == "T":
                    i = s[1]
                    kts = items[i][3]
                    for hh in range(2):
                        pe.wait_ge(pn_ready, 2 * i + hh + 1)
                        for a in range(0, len(kts), 4):
                            n = min(4, len(kts) - a)
                            b = bank(s, (hh, a))
                            for q in range(n):
                                ins = pe.transpose(b[:, q * P:(q + 1) * P], Pb[:, i % 2, hh, (a + q) * P:(a + q + 1) * P],
                                                   ident[:])
                            ins.then_inc(t_done, 1)
                if k == "PV":
                    i = s[1]
                    br, j, qt, kts = items[i]
                    for job in t_jobs(("T", i), items):
                        pe.wait_ge(*freed[job_at[job]])
                    if i >= 1:
                        pe.wait_ge(o_done, i)
                    for n, kt in enumerate(kts):
                        for hh in range(2):
                            ins = pe.matmul(ps[hh * 64:hh * 64 + 64, 4, 0:P], V[:, br, kt, hh * 64:hh * 64 + 64],
                                            PT[:, hh, n, :], start=(n == 0), stop=(n == len(kts) - 1),
                                            tile_position=(0, 64 * hh))
                    ins.then_inc(pv_done, 1)
                if k == "GT":
                    b = bank(s)
                    pe.wait_ge(dg_ready, s[1] + 1)
                    for q in range(4):
                        ins = pe.matmul(b[:, q * P:(q + 1) * P], ones[:], dg[:, s[1] % 2, q, :], start=(q == 0), stop=True,
                                        skip_group_check=True)
                    ins.then_inc(t_done, 1)
                if k == "M":
                    m, c = s[1], s[2]
                    n = m * 3 + c
                    w = 256 if c == 2 else 512
                    if n == 0:
                        drained()
                        pe.wait_ge(o_done, NI)
                        pe.wait_ge(e_done, 2 * NI)
                    if c == 0:
                        pe.wait_ge(mw_in[m % 2], 96 * (m // 2 + 1))
                    if n >= 2:
                        pe.wait_ge(mm_ready, n - 1)
                    o = mw[m % 2]
                    for b in range(2):
                        wg = at(o + 1024 * b, KD, P)
                        for kk in range(KD):
                            pe.matmul(ps[:, 4 * (n % 2) + b, 0:w], wg[:, kk, :], hT[:, kk, c * 512:c * 512 + w],
                                      start=(kk == 0), stop=(kk == KD - 1))
                    for b in range(2):
                        wb = at(o + 2048 + 512 * b, NPAIR, P)
                        for kk in range(NPAIR):
                            ins = pe.matmul(ps[:, 4 * (n % 2) + 2 + b, 0:w], wb[:, kk, :], qT[:, b, kk, c * 512:c * 512 + w],
                                            start=(kk == 0), stop=(kk == NPAIR - 1))
                    ins.then_inc(m_done, 1)
                if k == "O":
                    t = s[1]
                    if t == 0:
                        pe.wait_ge(mm_ready, 3 * KD)
                        pe.wait_ge(merged_ready, 3 * KD)
                    if t >= 2:
                        pe.wait_ge(out_free, t - 1)
                    for h in range(2):
                        pe.wait_ge(wo_in[h], 16)
                        for kk in range(KD):
                            ins = pe.matmul(ps[:, 2 * (t % 2) + h], merged[:, kk, t * P:(t + 1) * P], wo[h][:, kk, :],
                                            start=(kk == 0), stop=(kk == KD - 1))
                    ins.then_inc(out_done, 1)
                if k == "RT":
                    t = s[1]
                    jx = job_at[(("X2", t), 1)]
                    pe.wait_ge(*freed[jx])
                    pe.wait_ge(*freed[jx - 1])
                    if t >= 1:
                        pe.wait_ge(rexp, t)
                    if t == 0:
                        pe.wait_ge(table_in, 16 * 10)
                    for kk in range(KD):
                        ins = pe.matmul(ps[:, 4, 0:NE], h2T[t % 2][:, kk, :], wr[:, kk, :], start=(kk == 0), stop=(kk == KD - 1))
                    ins.then_inc(r_done, 1)
                if k == "AT":
                    t = s[1]
                    pe.wait_ge(aff_ready, t + 1)
                    b = bank(s)
                    pe.transpose(b[0:NE, 0:P], af[:, t % 2], ident[:]).then_inc(t_done, 1)
                if k == "I":
                    pe.wait_ge(topk_ready, 2)
                    for n in range(4):
                        b = bank(s, n)
                        g, what = n // 2, n % 2
                        c = (CAP_P, CAP_S)[g]
                        pe.transpose(b[0:c, 0:NE], (top if what else tif)[g][:], ident[0:NE, 0:NE]).then_inc(t_done, 1)

            def xe_transposes():
                for b3 in range(3):
                    for d in range(3 * b3, min(3 * b3 + 3, KD)):
                        o = (d - 3 * b3) * SLOTS
                        pe.transpose(ps[:, 5 + b3, o:o + CAP_S], xeS[:, d * P:(d + 1) * P], ident[:])
                        ins = pe.transpose(ps[:, 5 + b3, o + CAP_S:o + SLOTS], xeP[:, d * P:(d + 1) * P],
                                           ident[0:CAP_P, 0:CAP_P])
                    ins.then_inc(xe_done, 1)

            pe.wait_ge(idx_ready, 4)
            pe.wait_ge(gat[0], 16)
            pe.wait_ge(gat[1], 16)
            xe_transposes()
            with pe.Fori(0, NE) as e:
                pe.wait_ge(xe_ready, 3 * e + 3)
                for f in range(KF):
                    cg, cu = 2 * (f // 4), 2 * (f // 4) + 1
                    if f >= 3:
                        pe.wait_ge(hid_done, 16 * e + f - 2)
                    for half, c in enumerate((cg, cu)):
                        if f % 4 == 0:
                            pe.wait_ge(w_ld[c % 6], 32 * e + 16 * (c // 6) + 16)
                        wv = at(ring[c % 6], KD, 512)
                        for kk in range(KD):
                            ins = pe.matmul(ps[:, f % 3, half * SLOTS:(half + 1) * SLOTS],
                                            wv[:, kk, (f % 4) * P:(f % 4 + 1) * P], xeT[:, kk, :],
                                            start=(kk == 0), stop=(kk == KD - 1))
                    ins.then_inc(gu_done, 1)
                pe.wait_ge(hid_done, 16 * e + 16)
                pe.wait_ge(ye_done, 4 * e + 1)
                for d in range(KD):
                    c = 8 + d // 2
                    if d % 2 == 0:
                        pe.wait_ge(w_ld[c % 6], 32 * e + 32)
                    if d >= 2:
                        pe.wait_ge(yT_done, 8 * e + d - 1)
                    wv = at(ring[c % 6], KF, 256)
                    for kf in range(KF):
                        ins = pe.matmul(ps[:, 3 + d % 2, 0:SLOTS], wv[:, kf, (d % 2) * P:(d % 2 + 1) * P], hidT[:, kf, :],
                                        start=(kf == 0), stop=(kf == KF - 1))
                    ins.then_inc(dn_done, 1)
                pe.wait_ge(gat[0], 16 * e + 32)
                pe.wait_ge(gat[1], 16 * e + 32)
                xe_transposes()
                pe.wait_ge(yT_done, 8 * e + 8)
                for n, (g, half, bk) in enumerate(((1, 0, 3), (1, 1, 4), (0, 0, 5), (0, 1, 6))):
                    if n == 2:
                        pe.wait_ge(xe_ready, 3 * e + 6)
                    a, z = ((CAP_S, SLOTS), (0, CAP_S))[g]
                    for q in range(4):
                        ins = pe.transpose(ps[0:z - a, bk, q * P:(q + 1) * P], yeT[:, half * 4 + q, a:z], ident[:])
                    ins.then_inc(yt_done, 1)


_INS = ["x_prompt", "x_sample", "c_prompt", "c_sample", "w_ada", "b_ada", "norm1_g", "w_in", "q_norm_g", "k_norm_g",
        "sink", "w_branch_a", "w_branch_b", "w_out", "norm2_g", "w_router", "w_e_gate", "w_e_up", "w_e_down",
        "rel_bias", "norm_f_g"]


def kernel(**inputs):
    import concourse.bacc as _bacc
    from concourse.bass_utils import run_bass_kernel_spmd as _run

    nc = _bacc.Bacc("TRN2", target_bir_lowering=False, num_devices=1)
    arrays, args = {}, []
    cos, sin = rope_tables()
    for name, a in [(n, inputs[n]) for n in _INS] + [("rope_c", cos), ("rope_s", sin), ("onehot", bucket_onehot())]:
        a = np.ascontiguousarray(a)
        arrays[name] = a
        args.append(nc.dram_tensor(name, a.shape, mybir.dt.from_np(a.dtype), kind="ExternalInput").ap())
    for name, shape in (("y_prompt", (1, SEQ, D)), ("y_sample", (1, DEC, D))):
        args.append(nc.dram_tensor(name, shape, F32, kind="ExternalOutput").ap())
    encoder(nc, *args)
    r = _run(nc, [arrays], core_ids=[0])
    return r.results[0]["y_prompt"], r.results[0]["y_sample"]
```

```python
from contextlib import ExitStack

import numpy as np

import concourse.bass as bass
from concourse import mybir

F32 = mybir.dt.float32
BF16 = mybir.dt.bfloat16
U32 = mybir.dt.uint32
ALU = mybir.AluOpType
ACT = mybir.ActivationFunctionType
AX = mybir.AxisListType

P = 128
D = 1024
KD = D // P
SEQ, DEC = 256, 1024
TOK = SEQ + DEC
NT = TOK // P
PT_TILES = SEQ // P
HD = 64
NPAIR = 4
QKV = 1536
WIN = 128
N_BUCKETS, MAX_DISTANCE = 32, 128
GRID_W, THETA = 64, 10000.0
NE = 16
CAP_S, CAP_P = 2 * DEC // NE, 2 * SEQ // NE
SLOTS = CAP_S + CAP_P
FF = 2048
KF = FF // P
EPS = 1e-6
NEG = -1e30
RELW = 511
CH = 4096


def rope_tables():
    t = np.arange(DEC)
    inv = (THETA ** (-np.arange(0, 32, 2, dtype=np.float32) / np.float32(32))).astype(np.float32)
    row = (t // GRID_W).astype(np.float32)[:, None] * inv
    col = (t % GRID_W).astype(np.float32)[:, None] * inv
    c = np.concatenate([np.cos(row), np.cos(row), np.cos(col), np.cos(col)], 1).astype(np.float32)
    s = np.concatenate([-np.sin(row), np.sin(row), -np.sin(col), np.sin(col)], 1).astype(np.float32)
    return tuple(np.ascontiguousarray(x.reshape(8, P, HD).transpose(1, 0, 2)) for x in (c, s))


def bucket_onehot():
    rel = np.arange(RELW) - 255
    half = N_BUCKETS // 2
    exact = half // 2
    n = np.abs(rel)
    large = exact + (np.log(np.maximum(n, 1).astype(np.float32) / np.float32(exact))
                     / np.float32(np.log(MAX_DISTANCE / exact)) * np.float32(half - exact)).astype(np.int32)
    b = (rel > 0) * half + np.where(n < exact, n, np.minimum(large, half - 1))
    m = np.zeros((33, RELW), np.float32)
    m[b, np.arange(RELW)] = 1.0
    m[:, n > WIN] = 0.0
    m[32, n > WIN] = 1.0
    return m


def group_of(t):
    return 0 if t < PT_TILES else 1


def attention_items():
    items = []
    for br in (0, 1):
        for lo, hi in ((0, PT_TILES), (PT_TILES, NT)):
            for qt in range(lo, hi):
                kts = list(range(lo, hi)) if br == 0 else list(range(max(lo, qt - 1), min(hi, qt + 2)))
                items += [(br, j, qt, kts) for j in range(NPAIR)]
    return items


def plan_steps(items):
    s = [("vec",)] + [("br", h) for h in range(8)]
    s += [("XP", 0), ("XP", 1), ("AR", 0), ("AR", 1), ("AC", 0), ("AR", 2), ("AC", 1), ("AR", 3), ("AC", 2),
          ("AC", 3), ("A1",), ("X", 0), ("XP", 2), ("X", 1), ("tab",)]
    for t in range(NT):
        s.append(("G", t))
        if t + 2 < NT:
            s.append(("X", t + 2))
        if t >= 1:
            s.append(("Q", t - 1))
        s.append(("N", t))
        if t + 3 < NT:
            s.append(("XP", t + 3))
    s.append(("Q", NT - 1))
    c, t, pv = 4, 0, 0
    first_b = next(i for i, x in enumerate(items) if x[0] == 1)
    for i in range(len(items) + 2):
        if i < len(items):
            s.append(("S", i))
        if t <= i - (1 if i <= first_b else 2):
            s.append(("T", t))
            t += 1
        if i < len(items):
            s.append(("R", i))
        if pv <= t - 2:
            s.append(("PV", pv))
            pv += 1
        if i >= 12 and i % 5 == 0 and c < 12:
            s += [("AR", c), ("AC", c)]
            c += 1
    s += [("PV", pv), ("A2",)]
    assert t == len(items) and pv == len(items) - 1
    s.append(("HS", 0))
    s += [("GT", n) for n in range(4)]
    s += [("WS", 0), ("HS", 1), ("HS", 2)]
    for m in range(KD):
        s.append(("M", m, 0))
        if m + 1 < KD:
            s.append(("WS", m + 1))
        s += [("M", m, 1), ("M", m, 2)]
    for t in range(NT + 3):
        if t < NT:
            s.append(("O", t))
        if 0 <= t - 1 < NT:
            s.append(("X2", t - 1))
        if 0 <= t - 2 < NT:
            s.append(("RT", t - 2))
        if 0 <= t - 3 < NT:
            s.append(("AT", t - 3))
        if t == 6:
            s.append(("K", 0))
        if t < NT:
            s.append(("XO", t))
    s += [("GT", n) for n in range(4, 8)]
    s += [("K", 1), ("I",)]
    return s


def t_jobs(step, items):
    k = step[0]
    if k in ("X", "X2"):
        return [(step, 0), (step, 1)]
    if k == "Q":
        return [(step, n) for n in range(3)]
    if k in ("vec", "br", "AR", "AC", "GT", "AT"):
        return [(step, 0)]
    if k == "T":
        return [(step, (hh, a)) for hh in range(2) for a in range(0, len(items[step[1]][3]), 4)]
    if k == "I":
        return [(step, n) for n in range(4)]
    return []


def encoder(nc, x_p, x_s, c_p, c_s, w_ada, b_ada, n1g, w_in, qg, kg, sink, w_ba, w_bb, w_out, n2g, w_router,
            w_gate, w_up, w_down, rel_bias, nfg, rope_c, rope_s, onehot, y_p, y_s):
    items = attention_items()
    NI = len(items)
    steps = plan_steps(items)
    jobs = [j for s in steps for j in t_jobs(s, items)]
    job_at = {j: n for n, j in enumerate(jobs)}

    x_d = [x_p[0], x_s[0]]
    y_d = [y_p[0], y_s[0]]
    ada_v = w_ada[0].rearrange("(k p) n -> p k n", p=P)
    win_v = w_in[0].rearrange("(k p) n -> p k n", p=P)
    wout_v = w_out[0].rearrange("(k p) n -> p k n", p=P)
    wbr_v = [w[0].rearrange("(v j p) n -> v p j n", v=2, j=NPAIR) for w in (w_ba, w_bb)]

    acc_d = [nc.dram_tensor("acc_prompt", [SEQ, D], F32).ap(), nc.dram_tensor("acc_sample", [DEC, D], F32).ap()]
    xn_d = [nc.dram_tensor("xn_prompt", [SEQ, D], F32).ap(), nc.dram_tensor("xn_sample", [DEC, D], F32).ap()]
    brow_d = nc.dram_tensor("bias_rows", [P * 8 * RELW + 8], F32)

    def token_rows(d, t):
        g = group_of(t)
        r = (t - (PT_TILES if g else 0)) * P
        return d[g][r:r + P, :]

    with ExitStack() as ctx:
        def sb(name, shape, dt=F32):
            return ctx.enter_context(nc.sbuf_tensor(name, shape, dt))

        def sem(name):
            return ctx.enter_context(nc.semaphore(name))

        arena = sb("arena", [P, 50688])

        def at(o, *dims):
            n = int(np.prod(dims))
            v = arena[:, o:o + n]
            if len(dims) == 2:
                v = v.rearrange("p (a b) -> p a b", a=dims[0])
            if len(dims) == 3:
                v = v.rearrange("p (a b c) -> p a b c", a=dims[0], b=dims[1])
            if len(dims) == 4:
                v = v.rearrange("p (a b c d) -> p a b c d", a=dims[0], b=dims[1], c=dims[2])
            return v

        def half_words(o, *dims):
            v = arena[:, o:o + int(np.prod(dims)) // 2].bitcast(BF16)
            if len(dims) == 2:
                return v.rearrange("p (a b) -> p a b", a=dims[0])
            return v.rearrange("p (a b c) -> p a b c", a=dims[0], b=dims[1])

        hT = at(0, KD, TOK)
        qT = at(10240, 2, NPAIR, TOK)
        kz = at(20480, 2, 2, TOK)
        V = at(25600, 2, NT, P)
        R3, R4 = 28160, 40448
        ada_slot = {c: o for c, o in enumerate([0, 4096, 10240, 14336])}
        ada_slot.update({c: R3 + CH * (c % 2) for c in range(4, 12)})
        wqkv = [at(R3 + CH * c, KD, 512) for c in range(3)]
        brow = at(20480, 8, RELW)
        relb = at(26700, 8, P)[0:33]
        oneh = at(24600, RELW)[0:33]
        xt = at(R4, 2, D)
        xn = at(R4 + 2048, 2, D)
        raw = at(R4 + 4096, QKV)
        rawB = raw[:, 768:1280].rearrange("p (j v d) -> p j v d", j=NPAIR, v=2)
        sq = at(R4 + 5632, 10, HD)
        t2 = at(R4 + 6272, 10, HD)
        qf = at(R4 + 6912, 2, 10, HD)
        tabs = at(R4 + 8192, 4, 8, HD)
        modrow0 = at(R4 + 6912, 2, 512)
        Pb = at(R4, 2, 2, 1024)
        PbB = at(R4, 8, 384).rearrange("p (i h) w -> p i h w", h=2)
        PT = at(R3 + 2 * CH, 2, 2, 8, P)
        biasm = at(R4 + 6144, 8, 384)
        modrow1 = at(R4 + 9216, 2, 512)
        dg = at(R4, 2, 4, P)
        oT = half_words(10240, 2 * NPAIR, NT, 2 * P)
        hTs = half_words(R3, 2 * KD, TOK)
        merged = at(0, KD, TOK)
        MW = 3 * KD * P
        mw = 20480
        mws = [mw + MW, 42496]
        wo = [at(38400, KD, 512), at(38400 + CH, KD, 512)]
        sig = at(46592, 2, 2, 512)
        gt1b = at(48640, 2, D)
        xo = at(20480, 2, D)
        x1 = at(22528, 2, D)
        xn2 = at(24576, 2, D)
        h2T = [at(26624, KD, P), at(46592, KD, P)]
        affS = at(47616, DEC)[0:NE]
        stage = [0, CH, 2 * CH]
        split = [3 * CH, 4 * CH, 5 * CH, 6 * CH, 7 * CH, 46592]
        B = 8 * CH
        hidT = half_words(B, 2, KF, SLOTS)
        xeT = half_words(B + 2560, 2, KD, SLOTS)
        yeT = at(B + 3840, KD, SLOTS)
        xeS, xeP = at(B + 5120, D), at(B + 6144, D)[0:CAP_P]
        yeS, yeP = at(B + 7168, D), at(B + 8192, D)[0:CAP_P]
        gt2b = at(B + 9216, 2, D)
        sil = at(B + 11264, 2, SLOTS)
        xe32 = at(B + 11584, KD, SLOTS)
        hid32 = at(B + 12864, 4, SLOTS)
        nfb = at(2 * NT * D, D)
        fin = at(0, NT, D)
        finy = at(10240, NT, D)

        ident = sb("ident", [P, P])
        ones = sb("ones", [P, P])
        vec = sb("vec", [80, P])
        spare = sb("spare", [P, 1])
        vecT = sb("vecT", [P, 80])
        modT = sb("modT", [P, 48, 2])
        A1 = sb("A1", [P, KD, 2])
        A2 = sb("A2", [P, KD, 2])
        cS = sb("cS", [P, KD, 32])
        sel = sb("sel", [P, 2])
        wr = sb("wr", [P, KD, NE])
        gains = sb("gains", [P, 2, HD])
        snk = sb("snk", [P, 8])
        nsnk = sb("nsnk", [P, 8])
        relc = sb("relc", [32, 8])
        st = sb("st", [P, 4, 2, 8])
        rs = sb("rs", [P, 2, 8])
        qs = sb("qs", [P, 5, 10])
        affP = sb("affP", [NE, SEQ])
        lg = sb("lg", [P, 2, NE])
        af = sb("af", [P, 2, NE])
        rst = sb("rst", [P, 2, 4])
        top = [sb("top_p", [NE, CAP_P]), sb("top_s", [NE, CAP_S])]
        ti = [sb("ti_p", [NE, CAP_P], U32), sb("ti_s", [NE, CAP_S], U32)]
        tif = [sb("tif_p", [NE, CAP_P]), sb("tif_s", [NE, CAP_S])]
        idx = [sb("idx_p", [CAP_P, NE], U32), sb("idx_s", [CAP_S, NE], U32)]
        gv = [sb("gv_p", [CAP_P, NE]), sb("gv_s", [CAP_S, NE])]
        gidx = [sb("gidx_p", [CAP_P, 1], U32), sb("gidx_s", [CAP_S, 1], U32)]
        sidx = [sb("sidx_p", [CAP_P, 1], U32), sb("sidx_s", [CAP_S, 1], U32)]
        ps = ctx.enter_context(nc.psum_tensor("ps", [P, 8, 512], F32))

        small_in, table_in = sem("small_in"), sem("table_in")
        ada_in = [sem(f"ada_in{n}") for n in range(6)]
        win_in = sem("win_in")
        x_in = [sem(f"x_in{n}") for n in range(2)]
        bias_out, bias_in = sem("bias_out"), sem("bias_in")
        const = sem("const")
        relb_ready = sem("relb_ready")
        kz_zero = sem("kz_zero")
        t_done = sem("t_done")
        t_free = [sem(f"t_free{n}") for n in range(3)]
        cs_ready = sem("cs_ready")
        modrow_ready, mod_ready = sem("modrow_ready"), sem("mod_ready")
        brow_ready = sem("brow_ready")
        chain = sem("chain")
        ssq = sem("ssq")
        rms_in, rms_sqrt = sem("rms_in"), sem("rms_sqrt")
        xn_ready = sem("xn_ready")
        g_done, g_free = sem("g_done"), [sem(f"g_free{n}") for n in range(5)]
        q_in, q_sqrt, qf_ready = sem("q_in"), sem("q_sqrt"), sem("qf_ready")
        s_done, nm_ready, e_done, es_done = sem("s_done"), sem("nm_ready"), sem("e_done"), sem("es_done")
        b_done = sem("b_done")
        rinv_ready = sem("rinv_ready")
        pn_pool, pn_vec = sem("pn_pool"), sem("pn_vec")
        pv_done, o_done = sem("pv_done"), sem("o_done")
        dg_ready, gt_ready = sem("dg_ready"), sem("gt_ready")
        o_hi, hs_hi, hs_done, ws_hi, ws_done = sem("o_hi"), sem("hs_hi"), sem("hs_done"), sem("ws_hi"), sem("ws_done")
        mw_in, wo_in = [sem("mw_in0"), sem("mw_in1")], [sem("wo_in0"), sem("wo_in1")]
        m_done, sig_ready, mm_ready, merged_ready = sem("m_done"), sem("sig_ready"), sem("mm_ready"), sem("merged_ready")
        out_done, out_free = sem("out_done"), sem("out_free")
        xo_in = [sem("xo_in0"), sem("xo_in1")]
        x1_ready, xn2_ready = sem("x1_ready"), sem("xn2_ready")
        x1_out, xn2_out = [sem("x1_out0"), sem("x1_out1")], [sem("xn2_out0"), sem("xn2_out1")]
        r_done, rmax, rexp, aff_ready = sem("r_done"), sem("rmax"), sem("rexp"), sem("aff_ready")
        topk_ready, idx_ready = sem("topk_ready"), sem("idx_ready")
        w_ld = [sem(f"w_ld{n}") for n in range(3)]
        hi_done, lo_done = sem("hi_done"), sem("lo_done")
        prod_done, hid_done = sem("prod_done"), sem("hid_done")
        xe_mod = sem("xe_mod")
        nf_in = sem("nf_in")
        cidx, high = sem("cidx"), sem("high")
        gat = [sem("gat_p"), sem("gat_s")]
        sca = [sem("sca_p"), sem("sca_s")]
        xe_done, xe_ready = sem("xe_done"), sem("xe_ready")
        gu_done, sil_done = sem("gu_done"), sem("sil_done")
        dn_done, yT_done = sem("dn_done"), sem("yT_done")
        yt_done, ye_done, gated = sem("yt_done"), sem("ye_done"), sem("gated")
        f_in = [sem(f"f_in{n}") for n in range(NT)]
        f_ss, f_v, f_sq, y_ready, y_out = sem("f_ss"), sem("f_v"), sem("f_sq"), sem("y_ready"), sem("y_out")

        def bank_of(n):
            return 5 + n % 3

        def stage_half(h):
            return at(stage[h // 2 % 3] + CH // 2 * (h % 2), CH // 2)

        def split_half(h):
            parts = half_words(split[h // 2 % 6], 2, CH)
            return [parts[:, n, CH // 2 * (h % 2):CH // 2 * (h % 2 + 1)] for n in range(2)]

        AHEAD = 8
        xe_groups = [(0, 3), (3, 6), (6, 8)]

        n_exp = lambda i, hh: 2 * i + hh + 1

        by_vec = lambda i, hh: items[i][0] == 0 and hh == 1
        n_norm = lambda i, hh: sum(by_vec(x, y) == by_vec(i, hh) for x in range(i + 1) for y in range(2)
                                   if (x, y) <= (i, hh))

        def probs(i, hh):
            w = len(items[i][3]) * P
            return (Pb[:, i % 2, hh] if items[i][0] == 0 else PbB[:, i % 4, hh])[:, 0:w]

        n_add = lambda i, hh: 2 * sum(1 for x in items[:i] if x[0] == 1) + hh + 1

        block = ctx.enter_context(nc.Block())

        @block.sync
        def _(sp):
            rows = [(0, 8, c_p[0].rearrange("(r p) -> r p", p=P)), (8, 8, c_s[0].rearrange("(r p) -> r p", p=P)),
                    (16, 48, b_ada[0].rearrange("(r p) -> r p", p=P)),
                    (64, 8, n1g[0].rearrange("(r p) -> r p", p=P)), (72, 8, n2g[0].rearrange("(r p) -> r p", p=P))]
            for r, n, src in rows:
                sp.dma_start(vec[r:r + n, :], src).then_inc(small_in, 16)
            sp.dma_start(relc[:], rel_bias).then_inc(small_in, 16)
            sp.dma_start(oneh, onehot).then_inc(small_in, 16)
            for t in range(2):
                sp.dma_start(xt[:, t], token_rows(x_d, t)).then_inc(x_in[t], 16)
            for c in range(4):
                sp.dma_start(at(ada_slot[c], KD, 512), ada_v[:, :, c * 512:(c + 1) * 512]).then_inc(ada_in[c], 16)
            sp.dma_start(gains[:, 0], qg[0].partition_broadcast(P)).then_inc(table_in, 16)
            sp.dma_start(gains[:, 1], kg[0].partition_broadcast(P)).then_inc(table_in, 16)
            sp.dma_start(snk[:], sink[0].partition_broadcast(P)).then_inc(table_in, 16)
            sp.dma_start(tabs[:, 0], rope_c).then_inc(table_in, 16)
            sp.dma_start(tabs[:, 1], rope_s).then_inc(table_in, 16)
            sp.dma_start(tabs[:, 2], rope_c).then_inc(table_in, 16)
            sp.dma_start(tabs[:, 3], rope_s).then_inc(table_in, 16)
            for k in range(3):
                a, b = [(0, 3), (3, 6), (6, 8)][k]
                sp.dma_start(wr[:, a:b, :], w_router[0].rearrange("(k p) e -> p k e", p=P)[:, a:b, :])\
                    .then_inc(table_in, 16)
            for c in range(3):
                sp.dma_start(wqkv[c], win_v[:, :, c * 512:(c + 1) * 512]).then_inc(win_in, 16)
            sp.wait_ge(brow_ready, 8)
            sp.dma_start(brow_d.ap()[0:P * 8 * RELW].rearrange("(p n) -> p n", p=P),
                         brow.rearrange("p h r -> p (h r)")).then_inc(bias_out, 16)
            for t in range(2, NT):
                sp.wait_ge(xn_ready, t - 1)
                sp.dma_start(xt[:, t % 2], token_rows(x_d, t)).then_inc(x_in[t % 2], 16)
            sp.wait_ge(g_done, 3 * NT)
            for c in range(4, 6):
                sp.dma_start(at(ada_slot[c], KD, 512), ada_v[:, :, c * 512:(c + 1) * 512]).then_inc(ada_in[4 + c % 2], 16)
            sp.wait_ge(bias_out, 16)
            sp.wait_ge(t_done, job_at[(("Q", NT - 1), 2)] + 1)
            skew = bass.AP(tensor=brow_d, offset=127, ap=[[8 * RELW - 1, P], [RELW, 8], [1, 384]])
            sp.dma_start(biasm, skew).then_inc(bias_in, 16)
            for c in range(6, 12):
                sp.wait_ge(t_done, job_at[(("AR", c - 2), 0)] + 1)
                sp.dma_start(at(ada_slot[c], KD, 512), ada_v[:, :, c * 512:(c + 1) * 512]).then_inc(ada_in[4 + c % 2], 16)
            sp.wait_ge(pv_done, NI)
            for m in range(KD):
                if m >= 1:
                    sp.wait_ge(ws_done, m)
                w = mw
                for b in range(2):
                    c0 = QKV + b * D + m * P
                    sp.dma_start(at(w + 1024 * b, KD, P), win_v[:, :, c0:c0 + P]).then_inc(mw_in[m % 2], 16)
                    for v in range(2):
                        sp.dma_start(at(w + 2048 + 512 * b, NPAIR, P)[v * 64:v * 64 + 64],
                                     wbr_v[b][v][:, :, m * P:(m + 1) * P]).then_inc(mw_in[m % 2], 16)
                if m == 1:
                    sp.wait_ge(gt_ready, 4)
                    sp.dma_start(wo[0], wout_v[:, :, 0:512]).then_inc(wo_in[0], 16)
            sp.wait_ge(m_done, 3 * KD)
            sp.dma_start(wo[1], wout_v[:, :, 512:1024]).then_inc(wo_in[1], 16)
            sp.wait_ge(mm_ready, 3 * KD)

            def chunk_src(e, c):
                if c < 8:
                    w = (w_gate, w_up)[c % 2]
                    return w[0, e].rearrange("(k p) n -> p k n", p=P)[:, :, (c // 2) * 512:(c // 2 + 1) * 512]
                return w_down[0, e].rearrange("(k p) n -> p k n", p=P)[:, :, (c - 8) * 256:(c - 7) * 256]

            def load_chunk(e, c):
                dst = at(stage[c % 3], KD, 512) if c < 8 else at(stage[c % 3], KF, 256)
                sp.dma_start(dst, chunk_src(e, c)).then_inc(w_ld[c % 3], 16)

            for t in range(2):
                sp.dma_start(xo[:, t], token_rows(x_d, t)).then_inc(xo_in[t], 16)
            for t in range(NT):
                if t + 2 < NT:
                    sp.wait_ge(x1_ready, t + 1)
                    sp.dma_start(xo[:, t % 2], token_rows(x_d, t + 2)).then_inc(xo_in[t % 2], 16)
            sp.wait_ge(out_done, NT)
            for c in range(3):
                load_chunk(0, c)

            def load_after(e, c):
                if c == 4:
                    return
                sp.wait_ge(lo_done, 24 * e + 2 * c + 2)
                if c == 5:
                    load_chunk(e, 7)
                if c < 9:
                    load_chunk(e, c + 3)
                else:
                    load_chunk(e + 1, c - 9)

            with sp.Fori(0, NE - 1) as e:
                for c in range(12):
                    load_after(e, c)
            for c in range(9):
                load_after(NE - 1, c)
            sp.wait_ge(dn_done, 8 * NE)
            sp.wait_ge(sca[0], 16 * NE)
            sp.wait_ge(sca[1], 16 * NE)
            sp.dma_start(nfb, nfg.partition_broadcast(P)).then_inc(nf_in, 16)
            for t in range(NT):
                sp.dma_start(fin[:, t], token_rows(acc_d, t)).then_inc(f_in[t], 16)
            for t in range(NT):
                sp.wait_ge(y_ready, t + 1)
                sp.dma_start(token_rows(y_d, t), finy[:, t]).then_inc(y_out, 16)
            sp.wait_ge(y_out, 16 * NT)

        @block.gpsimd
        def _(gp):
            gp.memset(ident[:], 0.0).then_inc(const, 1)
            gp.memset(sel[:], 0.0).then_inc(const, 1)
            gp.memset(ones[:], 1.0).then_inc(const, 1)
            gp.memset(cS[:], 0.0).then_inc(const, 1)
            gp.wait_ge(const, 4)
            gp.affine_select(out=ident[:], in_=ident[:], compare_op=ALU.not_equal, fill=1.0, base=0,
                             pattern=[[-1, P]], channel_multiplier=1).then_inc(const, 1)
            for q in range(4):
                gp.affine_select(out=sel[:], in_=sel[:], compare_op=ALU.not_equal, fill=1.0, base=-32 * q,
                                 pattern=[[-1, 2]], channel_multiplier=1).then_inc(const, 1)
                gp.wait_ge(const, 6 + q)
            for s in steps:
                k = s[0]
                if k == "G" and s[1] == 0:
                    gp.wait_ge(bias_out, 16)
                    gp.wait_ge(t_done, job_at[(("AC", 3), 0)] + 1)
                    gp.memset(kz, 0.0).then_inc(kz_zero, 1)
                if k == "R":
                    i = s[1]
                    w = len(items[i][3]) * P
                    for hh in range(2):
                        if by_vec(i, hh):
                            continue
                        gp.wait_ge(rinv_ready, 2 * i + hh + 1)
                        p_ = probs(i, hh)
                        gp.tensor_scalar(p_, p_, st[:, i % 4, hh, 3:4], None, ALU.mult).then_inc(pn_pool, 1)
                if k == "M":
                    n = (s[1] * 3 + s[2])
                    w = 256 if s[2] == 2 else 512
                    gp.wait_ge(mm_ready, n + 1)
                    gp.tensor_tensor(merged[:, s[1], s[2] * 512:s[2] * 512 + w], sig[:, n % 2, 0, 0:w],
                                     sig[:, n % 2, 1, 0:w], ALU.add).then_inc(merged_ready, 1)
                if k in ("XO",):
                    t = s[1]
                    gp.wait_ge(xn2_ready, t + 1)
                    gp.dma_start(token_rows(xn_d, t), xn2[:, t % 2]).then_inc(xn2_out[t % 2], 16)
                    gp.dma_start(token_rows(acc_d, t), x1[:, t % 2]).then_inc(x1_out[t % 2], 16)

            def gather():
                for b, dst in ((1, xeS), (0, xeP)):
                    gp.indirect_dma_start(out=dst, out_offset=None, in_=xn_d[b],
                                          in_offset=bass.IndirectOffsetOnAxis(ap=gidx[b][:, 0:1], axis=0))\
                        .then_inc(gat[b], 16)

            def gate(n=None):
                if n is not None:
                    gp.wait_ge(gated, n)
                gp.tensor_tensor(spare[:, 0:1], ones[:, 0:1], ones[:, 1:2], ALU.add).then_inc(gated, 1)

            def split_rows(mods, highs):
                for n, (d0, d1) in enumerate(xe_groups):
                    gp.wait_ge(xe_mod, mods + n + 1)
                    gp.tensor_tensor(xeT[:, 0, d0:d1], xe32[:, d0:d1],
                                     ones[:, 0:d1 - d0].unsqueeze(2).to_broadcast([P, d1 - d0, SLOTS]), ALU.mult).then_inc(high, 1)
                    gp.wait_ge(high, highs + n + 1)
                    gp.tensor_tensor(xeT[:, 1, d0:d1], xe32[:, d0:d1], xeT[:, 0, d0:d1], ALU.subtract)\
                        .then_inc(xe_ready, 1)

            def split_hidden(e, f):
                gp.wait_ge(prod_done, 16 * e + f + 1)
                gp.tensor_tensor(hidT[:, 0, f], hid32[:, f % 4], ones[:, 0:1].to_broadcast([P, SLOTS]), ALU.mult).then_inc(high, 1)
                gp.wait_ge(high, 19 * e + f + 4)
                gp.tensor_tensor(hidT[:, 1, f], hid32[:, f % 4], hidT[:, 0, f], ALU.subtract).then_inc(hid_done, 1)

            for h in range(AHEAD):
                gp.wait_ge(hi_done, h + 1)
                hi, lo = split_half(h)
                gp.tensor_tensor(lo, stage_half(h), hi, ALU.subtract).then_inc(lo_done, 1)
            for b in range(2):
                gp.wait_ge(xn2_out[b], 16 * (NT // 2))
                gp.wait_ge(x1_out[b], 16 * (NT // 2))
            gp.wait_ge(idx_ready, 4)
            for b in range(2):
                gp.tensor_copy(gidx[b][:], idx[b][:, 0:1]).then_inc(cidx, 1)
            gp.wait_ge(cidx, 2)
            gather()
            gate()
            split_rows(0, 0)

            def expert_pool(e, last):
                c0, g0 = 4 * e + 2, 5 * e + 1
                if not last:
                    for b in range(2):
                        gp.wait_ge(gat[b], 16 * e + 16)
                    gp.wait_ge(xe_done, 3 * e + 3)
                    gate(g0)
                    for b in range(2):
                        gp.tensor_copy(gidx[b][:], idx[b][:, bass.ds(e + 1, 1)]).then_inc(cidx, 1)
                    gp.wait_ge(cidx, c0 + 2)
                    gate(g0 + 1)
                    gather()
                    c0, g0 = c0 + 2, g0 + 2
                for f in range(KF // 2):
                    split_hidden(e, f)
                for b in range(2):
                    gp.tensor_copy(sidx[b][:], idx[b][:, bass.ds(e, 1)]).then_inc(cidx, 1)
                gp.wait_ge(cidx, c0 + 2)
                gate(g0)
                for f in range(KF // 2, KF):
                    split_hidden(e, f)
                if not last:
                    split_rows(3 * e + 3, 19 * e + 19)
                gp.wait_ge(ye_done, 4 * e + 5)
                gate(g0 + 1)
                for b, src in ((1, yeS), (0, yeP)):
                    gp.indirect_dma_start(out=acc_d[b], out_offset=bass.IndirectOffsetOnAxis(ap=sidx[b][:, 0:1], axis=0),
                                          in_=src, in_offset=None, compute_op=ALU.add).then_inc(sca[b], 16)
                gp.wait_ge(sca[0], 16 * e + 16)
                gp.wait_ge(sca[1], 16 * e + 16)
                gate(g0 + 2)

            with gp.Fori(0, NE - 1) as e:
                expert_pool(e, False)
            expert_pool(NE - 1, True)

        @block.scalar
        def _(ac):
            def job(s, n=0):
                j = job_at[(s, n)]
                ac.wait_ge(t_done, j + 1)
                return ps[:, bank_of(j)], t_free[j % 3]

            def split_high(e, h):
                c = h // 2
                ac.wait_ge(w_ld[c % 3], 64 * e + 16 * (c // 3 + 1))
                ac.activation(split_half(h)[0], stage_half(h), ACT.Copy).then_inc(hi_done, 1)

            for s in steps:
                k = s[0]
                if k == "vec":
                    b, free = job(s)
                    ac.wait_ge(const, 4)
                    ac.activation(cS[:, :, 0:2].rearrange("p k g -> p g k"),
                                  b[:, 0:16].rearrange("p (g k) -> p g k", g=2), ACT.Silu).then_inc(cs_ready, 1)
                    ac.activation(vecT[:], b[:, 0:80], ACT.Copy).then_inc(free, 1)
                if k == "br":
                    b, free = job(s)
                    ac.activation(brow[:, s[1], :], b[:, 0:RELW], ACT.Copy).then_inc(brow_ready, 1)
                if k == "AR":
                    c = s[1]
                    b, free = job(s)
                    if c >= 2:
                        ac.wait_ge(t_done, job_at[(("AC", c - 2), 0)] + 1)
                    ac.activation((modrow0 if c < 4 else modrow1)[:, c % 2], b, ACT.Copy).then_inc(modrow_ready, 1)
                if k == "XP":
                    t = s[1]
                    ac.wait_ge(x_in[t % 2], 16 * (t // 2 + 1))
                    if t >= 2:
                        ac.wait_ge(t_done, job_at[(("X", t - 2), 1)] + 1)
                    ac.activation(xn[:, t % 2], xt[:, t % 2], ACT.Square, accum_out=rs[:, t % 2, 0:1]).then_inc(ssq, 1)
                    ac.wait_ge(rms_in, t + 1)
                    ac.activation(rs[:, t % 2, 2:3], rs[:, t % 2, 1:2], ACT.Sqrt).then_inc(rms_sqrt, 1)
                if k == "G":
                    t = s[1]
                    if t >= 1:
                        ac.wait_ge(t_done, job_at[(("Q", t - 1), 2)] + 1)
                        ac.wait_ge(qf_ready, t)
                    for c in range(3):
                        ac.wait_ge(g_done, 3 * t + c + 1)
                        n = 3 * t + c
                        b = ps[:, n % 5]
                        if c:
                            v0 = 128 if c == 1 else 384
                            if t == 0:
                                ac.wait_ge(kz_zero, 1)
                            ac.activation(V[:, c - 1, t, :], b[:, v0:v0 + P], ACT.Copy)
                        if c == 0:
                            ins = ac.activation(raw[:, 0:512], b, ACT.Copy)
                        elif c == 1:
                            ac.activation(raw[:, 512:640], b[:, 0:P], ACT.Copy)
                            ins = ac.activation(rawB[:, :, 0, :], b[:, 256:512].rearrange("p (j d) -> p j d", j=NPAIR),
                                                ACT.Copy)
                        else:
                            ac.activation(rawB[:, :, 1, :], b[:, 0:256].rearrange("p (j d) -> p j d", j=NPAIR), ACT.Copy)
                            ins = ac.activation(raw[:, 1280:1408], b[:, 256:384], ACT.Copy)
                        ins.then_inc(g_free[n % 5], 1)
                if k == "N":
                    t = s[1]
                    ac.wait_ge(q_in, t + 1)
                    ac.activation(qs[:, 2], qs[:, 1], ACT.Sqrt).then_inc(q_sqrt, 1)
                if k == "Q":
                    t = s[1]
                    for br in range(2):
                        b, free = job(s, br)
                        ac.activation(qT[:, br, :, t * P:(t + 1) * P], b.rearrange("p (j q) -> p j q", j=NPAIR),
                                      ACT.Copy, scale=1.0 if br == 0 else HD ** -0.5).then_inc(free, 1)
                if k == "S":
                    i = s[1]
                    br, j, qt, kts = items[i]
                    w = len(kts) * P
                    for hh in range(2):
                        h = j + 4 * hh
                        ac.wait_ge(nm_ready, 2 * i + hh + 1)
                        p_ = probs(i, hh)
                        src = p_ if br else ps[:, 2 * hh:2 * hh + 2].rearrange("p a b -> p (a b)")[:, 0:w]
                        ac.activation(p_, src, ACT.Exp, bias=st[:, i % 4, hh, 0:1],
                                      accum_out=st[:, i % 4, hh, 1:2]).then_inc(e_done, 1)
                        if br:
                            ac.activation(st[:, i % 4, hh, 2:3], snk[:, h:h + 1], ACT.Exp,
                                          bias=st[:, i % 4, hh, 0:1]).then_inc(es_done, 1)
                if k == "T":
                    i = s[1]
                    kts = items[i][3]
                    for a in range(0, len(kts), 4):
                        n = min(4, len(kts) - a)
                        b, free = job(s, (1, a))
                        ac.activation(PT[:, i % 2, 1, a:a + n, :], b[:, 0:n * P].rearrange("p (n q) -> p n q", n=n),
                                      ACT.Copy).then_inc(free, 1)
                if k == "PV":
                    i = s[1]
                    br, j, qt, kts = items[i]
                    ac.wait_ge(pv_done, i + 1)
                    ac.activation(oT[:, NPAIR * br + j, qt, 0:P], ps[:, 4, 0:P], ACT.Copy).then_inc(o_hi, 1)
                if k == "HS":
                    a, z = 512 * s[1], min(512 * s[1] + 512, TOK)
                    ac.activation(hTs[:, 0:KD, a:z], hT[:, :, a:z], ACT.Copy).then_inc(hs_hi, 1)
                if k == "WS":
                    m = s[1]
                    ac.wait_ge(mw_in[m % 2], 96 * (m // 2 + 1))
                    ac.activation(half_words(mws[m % 2], 2, MW)[:, 0], at(mw, MW), ACT.Copy).then_inc(ws_hi, 1)
                if k == "GT":
                    n = s[1]
                    b, free = job(s)
                    dst = (gt1b, gt2b)[n // 4]
                    ac.activation(dst[:, (n // 2) % 2, (n % 2) * 512:(n % 2) * 512 + 512], b, ACT.Copy)\
                        .then_inc(gt_ready, 1)
                if k == "K" and s[1] == 1:
                    for b in range(2):
                        ac.wait_ge(x1_out[b], 16 * (NT // 2))
                        ac.wait_ge(xn2_out[b], 16 * (NT // 2))
                    for h in range(AHEAD):
                        split_high(0, h)
                if k == "M":
                    n = s[1] * 3 + s[2]
                    w = 256 if s[2] == 2 else 512
                    ac.wait_ge(m_done, n + 1)
                    if n >= 2:
                        ac.wait_ge(merged_ready, n - 1)
                    for b in range(2):
                        ac.activation(sig[:, n % 2, b, 0:w], ps[:, 4 * (n % 2) + b, 0:w], ACT.Sigmoid)\
                            .then_inc(sig_ready, 1)
                if k == "XO":
                    t = s[1]
                    ac.wait_ge(x1_ready, t + 1)
                    if t >= 2:
                        ac.wait_ge(t_done, job_at[(("X2", t - 2), 1)] + 1)
                        ac.wait_ge(xn2_out[t % 2], 16 * (t // 2))
                    ac.activation(xn2[:, t % 2], x1[:, t % 2], ACT.Square, accum_out=rs[:, t % 2, 0:1]).then_inc(ssq, 1)
                    ac.wait_ge(rms_in, NT + t + 1)
                    ac.activation(rs[:, t % 2, 2:3], rs[:, t % 2, 1:2], ACT.Sqrt).then_inc(rms_sqrt, 1)
                if k == "RT":
                    t = s[1]
                    ac.wait_ge(rmax, t + 1)
                    ac.activation(lg[:, t % 2], ps[:, 4, 0:NE], ACT.Exp, bias=rst[:, t % 2, 0:1],
                                  accum_out=rst[:, t % 2, 1:2]).then_inc(rexp, 1)

            def expert_act(e, last):
                for u in range(KF + KD):
                    h = u + AHEAD
                    if not (last and h >= 24):
                        split_high(e, h)
                    if u < KF:
                        ac.wait_ge(gu_done, 16 * e + u + 1)
                        if u >= 2:
                            ac.wait_ge(prod_done, 16 * e + u - 1)
                        ac.activation(sil[:, u % 2], ps[:, u % 3, 0:SLOTS], ACT.Silu).then_inc(sil_done, 1)
                    else:
                        d = u - KF
                        ac.wait_ge(dn_done, 8 * e + d + 1)
                        ac.activation(yeT[:, d, :], ps[:, 3 + d % 2, 0:SLOTS], ACT.Copy).then_inc(yT_done, 1)

            with ac.Fori(0, NE - 1) as e:
                expert_act(e, False)
            expert_act(NE - 1, True)
            for t in range(NT):
                ac.wait_ge(f_in[t], 16)
                ac.activation(finy[:, t], fin[:, t], ACT.Square, accum_out=rs[:, t % 2, 4:5]).then_inc(f_ss, 1)
                ac.wait_ge(f_v, t + 1)
                ac.activation(rs[:, t % 2, 6:7], rs[:, t % 2, 5:6], ACT.Sqrt).then_inc(f_sq, 1)

        @block.vector
        def _(ve):
            count = [0]

            def link(ins):
                count[0] += 1
                ins.then_inc(chain, 1)
                ve.wait_ge(chain, count[0])

            def job(s, n=0):
                j = job_at[(s, n)]
                ve.wait_ge(t_done, j + 1)
                return ps[:, bank_of(j)], t_free[j % 3]

            def mod_affine(A, gain0, m):
                link(ve.tensor_scalar(A[:], modT[:, m:m + KD, :], 1.0, None, ALU.add))
                for g in range(2):
                    link(ve.tensor_tensor(A[:, :, g], A[:, :, g], vecT[:, gain0:gain0 + KD], ALU.mult))

            def norm_in(n):
                ve.wait_ge(ssq, n + 1)
                t = n % NT
                ve.tensor_scalar(rs[:, t % 2, 1:2], rs[:, t % 2, 0:1], 1.0 / D, EPS, ALU.mult, ALU.add).then_inc(rms_in, 1)
                ve.wait_ge(rms_sqrt, n + 1)
                link(ve.reciprocal(rs[:, t % 2, 3:4], rs[:, t % 2, 2:3]))

            def modulate(s, dst, A, sh, g):
                for half in range(2):
                    b, free = job(s, half)
                    for q in range(4):
                        kk = half * 4 + q
                        ins = ve.tensor_scalar(dst(kk), b[:, q * P:(q + 1) * P], A[:, kk, g:g + 1],
                                               modT[:, sh + kk, g:g + 1], ALU.mult, ALU.add)
                    ins.then_inc(free, 1)

            def topk(b, a):
                n = (CAP_P, CAP_S)[b] // 8
                for r in range(n):
                    v = top[b][:, r * 8:r * 8 + 8]
                    link(ve.max(v, a))
                    ve.max_index(ti[b][:, r * 8:r * 8 + 8], v, a)
                    link(ve.match_replace(a, v, a, -1.0))
                ve.tensor_copy(tif[b][:], ti[b][:]).then_inc(topk_ready, 1)

            ve.memset(relb, NEG).then_inc(chain, 1)
            count[0] += 1
            ve.wait_ge(chain, count[0])
            ve.wait_ge(small_in, 16 * 7)
            for h in range(8):
                ins = ve.tensor_copy(relb[0:32, h, :], relc[:, h:h + 1].to_broadcast([32, P]))
            ins.then_inc(relb_ready, 1)
            for s in steps:
                k = s[0]
                if k == "AC":
                    c = s[1]
                    b, free = job(s)
                    if c == 0:
                        ve.wait_ge(t_free[job_at[(("vec",), 0)] % 3], 1)
                    ve.tensor_tensor(modT[:, 4 * c:4 * c + 4, :], b[:, 0:8].rearrange("p (n g) -> p n g", n=4),
                                     vecT[:, 16 + 4 * c:20 + 4 * c].unsqueeze(2).to_broadcast([P, 4, 2]),
                                     ALU.add).then_inc(mod_ready, 1)
                if k == "A1":
                    ve.wait_ge(mod_ready, 4)
                    mod_affine(A1, 64, 8)
                if k == "A2":
                    ve.wait_ge(mod_ready, 12)
                    mod_affine(A2, 72, 32)
                if k == "tab":
                    ve.wait_ge(table_in, 16 * 10)
                    link(ve.tensor_scalar(nsnk[:], snk[:], -1.0, None, ALU.mult))
                    for n in range(2):
                        for x in range(8):
                            tc_, ts_ = tabs[:, 2 * n, x], tabs[:, 2 * n + 1, x]
                            ve.tensor_tensor(tc_, tc_, gains[:, n], ALU.mult)
                            for a in range(2):
                                ins = ve.tensor_tensor(
                                    ts_.rearrange("p (u a v) -> p u a v", u=2, a=2)[:, :, a],
                                    ts_.rearrange("p (u a v) -> p u a v", u=2, a=2)[:, :, a],
                                    gains[:, n].rearrange("p (u a v) -> p u a v", u=2, a=2)[:, :, 1 - a], ALU.mult)
                    link(ins)
                    link(ve.tensor_scalar(tabs[:, 0:2], tabs[:, 0:2], HD ** -0.5, None, ALU.mult))
                if k == "XP":
                    t = s[1]
                    norm_in(t)
                    ve.tensor_scalar(xn[:, t % 2], xt[:, t % 2], rs[:, t % 2, 3:4], None, ALU.mult).then_inc(xn_ready, 1)
                if k == "X":
                    t = s[1]
                    modulate(s, lambda kk: hT[:, kk, t * P:(t + 1) * P], A1, 0, group_of(t))
                if k == "N":
                    t = s[1]
                    for c in range(3):
                        n = 3 * t + c
                        ve.wait_ge(g_free[n % 5], n // 5 + 1)
                    rope_t = (t if t < PT_TILES else t - PT_TILES)
                    r10 = raw[:, 0:640].rearrange("p (h d) -> p h d", h=10)
                    link(ve.tensor_tensor(sq, r10, r10, ALU.mult))
                    link(ve.tensor_reduce(qs[:, 0], sq, AX.X, ALU.add))
                    ve.tensor_scalar(qs[:, 1], qs[:, 0], 1.0 / HD, EPS, ALU.mult, ALU.add).then_inc(q_in, 1)
                    ve.wait_ge(q_sqrt, t + 1)
                    link(ve.reciprocal(qs[:, 3], qs[:, 2]))
                    link(ve.tensor_tensor(qs[:, 4], qs[:, 3], qs[:, 3], ALU.mult))
                    link(ve.tensor_tensor(qs[:, 4], qs[:, 4], qs[:, 1], ALU.mult))
                    link(ve.tensor_scalar(qs[:, 4], qs[:, 4], -0.5, 1.5, ALU.mult, ALU.add))
                    link(ve.tensor_tensor(qs[:, 3], qs[:, 3], qs[:, 4], ALU.mult))
                    link(ve.tensor_tensor(sq, r10, qs[:, 3].unsqueeze(2).to_broadcast([P, 10, HD]), ALU.mult))
                    out = qf[:, t % 2]
                    for n, (a, z) in enumerate(((0, 8), (8, 10))):
                        tc_ = tabs[:, 2 * n, rope_t]
                        ve.tensor_tensor(r10[:, a:z], sq[:, a:z], tc_.unsqueeze(1).to_broadcast([P, z - a, HD]), ALU.mult)
                        for hf in range(2):
                            for u in range(2):
                                o1 = u * 32 + hf * 16
                                o2 = u * 32 + (1 - hf) * 16
                                ins = ve.tensor_tensor(
                                    t2[:, a:z, o1:o1 + 16], sq[:, a:z, o2:o2 + 16],
                                    tabs[:, 2 * n + 1, rope_t, o1:o1 + 16].unsqueeze(1).to_broadcast([P, z - a, 16]),
                                    ALU.mult)
                    link(ins)
                    ve.tensor_tensor(out[:, 0:8].rearrange("p (j v) d -> p v j d", v=2),
                                     r10[:, 0:8].rearrange("p (v j) d -> p v j d", v=2),
                                     t2[:, 0:8].rearrange("p (v j) d -> p v j d", v=2), ALU.add)
                    ve.tensor_tensor(out[:, 8:10], r10[:, 8:10], t2[:, 8:10], ALU.add).then_inc(qf_ready, 1)
                if k == "Q":
                    t = s[1]
                    if t == 0:
                        ve.wait_ge(kz_zero, 1)
                    b, free = job(s, 2)
                    for v in range(2):
                        r = slice(v * 64, v * 64 + 64)
                        ins = ve.tensor_copy(kz[r, :, v, t * P:(t + 1) * P],
                                             b[r, 0:256].rearrange("p (b q) -> p b q", b=2))
                    ins.then_inc(free, 1)
                if k == "S":
                    i = s[1]
                    br, j, qt, kts = items[i]
                    w = len(kts) * P
                    for hh in range(2):
                        h = j + 4 * hh
                        ve.wait_ge(s_done, 2 * i + hh + 1)
                        src = ps[:, 2 * hh:2 * hh + 2].rearrange("p a b -> p (a b)")[:, 0:w]
                        nm = st[:, i % 4, hh, 0:1]
                        if br == 0:
                            ve.tensor_reduce(nm, src, AX.X, ALU.max, negate=True).then_inc(nm_ready, 1)
                        else:
                            ve.wait_ge(bias_in, 16)
                            b0 = (kts[0] - qt + 1) * P
                            p_ = probs(i, hh)
                            ve.tensor_tensor(p_, src, biasm[:, h, b0:b0 + w], ALU.add).then_inc(b_done, 1)
                            ve.wait_ge(b_done, n_add(i, hh))
                            link(ve.tensor_reduce(nm, p_, AX.X, ALU.max, negate=True))
                            ve.tensor_tensor(nm, nm, nsnk[:, h:h + 1], ALU.min).then_inc(nm_ready, 1)
                if k == "R":
                    i = s[1]
                    br = items[i][0]
                    for hh in range(2):
                        ve.wait_ge(e_done, 2 * i + hh + 1)
                        f = st[:, i % 4, hh]
                        den = f[:, 1:2]
                        if br:
                            ve.wait_ge(es_done, n_add(i, hh))
                            link(ve.tensor_tensor(den, f[:, 1:2], f[:, 2:3], ALU.add))
                        ve.reciprocal(f[:, 3:4], den).then_inc(rinv_ready, 1)
                        if by_vec(i, hh):
                            p_ = probs(i, hh)
                            ve.wait_ge(rinv_ready, 2 * i + hh + 1)
                            ve.tensor_scalar(p_, p_, f[:, 3:4], None, ALU.mult).then_inc(pn_vec, 1)
                if k == "T":
                    i = s[1]
                    kts = items[i][3]
                    for a in range(0, len(kts), 4):
                        n = min(4, len(kts) - a)
                        b, free = job(s, (0, a))
                        ve.tensor_copy(PT[:, i % 2, 0, a:a + n, :], b[:, 0:n * P].rearrange("p (n q) -> p n q", n=n))\
                            .then_inc(free, 1)
                if k == "PV":
                    br, j, qt, kts = items[s[1]]
                    ve.wait_ge(o_hi, s[1] + 1)
                    o = oT[:, NPAIR * br + j, qt]
                    ve.tensor_tensor(o[:, P:2 * P], ps[:, 4, 0:P], o[:, 0:P], ALU.subtract).then_inc(o_done, 1)
                if k == "HS":
                    a, z = 512 * s[1], min(512 * s[1] + 512, TOK)
                    ve.wait_ge(hs_hi, s[1] + 1)
                    ve.tensor_tensor(hTs[:, KD:2 * KD, a:z], hT[:, :, a:z], hTs[:, 0:KD, a:z], ALU.subtract)\
                        .then_inc(hs_done, 1)
                if k == "WS":
                    m = s[1]
                    ve.wait_ge(ws_hi, m + 1)
                    w = half_words(mws[m % 2], 2, MW)
                    ve.tensor_tensor(w[:, 1], at(mw, MW), w[:, 0], ALU.subtract).then_inc(ws_done, 1)
                if k == "GT":
                    n = s[1]
                    if n % 4 >= 2:
                        ve.wait_ge(t_done, job_at[(("GT", n - 2), 0)] + 1)
                    m0, g = (16, 40)[n // 4], (n // 2) % 2
                    for q in range(4):
                        mm = m0 + (n % 2) * 4 + q
                        ins = ve.tensor_scalar(dg[:, n % 2, q, :], ident[:], modT[:, mm, g:g + 1], None, ALU.mult)
                    ins.then_inc(dg_ready, 1)
                if k == "M":
                    n = s[1] * 3 + s[2]
                    w = 256 if s[2] == 2 else 512
                    for b in range(2):
                        ve.wait_ge(sig_ready, 2 * n + 2)
                        x = sig[:, n % 2, b, 0:w]
                        ins = ve.tensor_tensor(x, x, ps[:, 4 * (n % 2) + 2 + b, 0:w], ALU.mult)
                    ins.then_inc(mm_ready, 1)
                if k == "XO":
                    t = s[1]
                    g = group_of(t)
                    ve.wait_ge(out_done, t + 1)
                    ve.wait_ge(xo_in[t % 2], 16 * (t // 2 + 1))
                    if t >= 2:
                        ve.wait_ge(x1_out[t % 2], 16 * (t // 2))
                    o = ps[:, 2 * (t % 2):2 * (t % 2) + 2].rearrange("p a b -> p (a b)")
                    ve.tensor_tensor(x1[:, t % 2], o, gt1b[:, g], ALU.mult).then_inc(out_free, 1)
                    ve.wait_ge(out_free, t + 1)
                    ve.tensor_tensor(x1[:, t % 2], x1[:, t % 2], xo[:, t % 2], ALU.add).then_inc(x1_ready, 1)
                    norm_in(NT + t)
                    ve.tensor_scalar(xn2[:, t % 2], x1[:, t % 2], rs[:, t % 2, 3:4], None, ALU.mult).then_inc(xn2_ready, 1)
                if k == "X2":
                    t = s[1]
                    modulate(s, lambda kk: h2T[t % 2][:, kk, :], A2, 24, group_of(t))
                if k == "RT":
                    t = s[1]
                    ve.wait_ge(r_done, t + 1)
                    ve.tensor_reduce(rst[:, t % 2, 0:1], ps[:, 4, 0:NE], AX.X, ALU.max, negate=True).then_inc(rmax, 1)
                    ve.wait_ge(rexp, t + 1)
                    link(ve.reciprocal(rst[:, t % 2, 2:3], rst[:, t % 2, 1:2]))
                    ve.tensor_scalar(af[:, t % 2], lg[:, t % 2], rst[:, t % 2, 2:3], None, ALU.mult).then_inc(aff_ready, 1)
                if k == "AT":
                    t = s[1]
                    b, free = job(s)
                    if t < PT_TILES:
                        dst = affP[:, t * P:(t + 1) * P]
                    else:
                        dst = affS[:, (t - PT_TILES) * P:(t - PT_TILES + 1) * P]
                    link(ve.tensor_copy(dst, b[0:NE, 0:P]))
                    ve.engine_nop().then_inc(free, 1)
                if k == "K":
                    topk(s[1], affP[:] if s[1] == 0 else affS)
                if k == "I":
                    for n in range(4):
                        b, free = job(s, n)
                        g, what = n // 2, n % 2
                        c = (CAP_P, CAP_S)[g]
                        dst = gv[g][:] if what else idx[g][:, 0:NE]
                        ve.tensor_copy(dst, b[0:c, 0:NE]).then_inc(idx_ready, 1)

            def modulate_rows(n0):
                for n, (d0, d1) in enumerate(xe_groups):
                    ve.wait_ge(xe_done, n0 + n + 1)
                    for d in range(d0, d1):
                        o = (d - d0) * SLOTS
                        for g, a, z in ((1, 0, CAP_S), (0, CAP_S, SLOTS)):
                            ins = ve.tensor_scalar(xe32[:, d, a:z], ps[:, 5 + n, o + a:o + z], A2[:, d, g:g + 1],
                                                   modT[:, 24 + d, g:g + 1], ALU.mult, ALU.add)
                    ins.then_inc(xe_mod, 1)

            modulate_rows(0)
            ve.memset(rst[:, 0, 0:1], 0.0).then_inc(ye_done, 1)
            ve.wait_ge(lo_done, AHEAD)

            def expert_vec(e, last):
                for u in range(KF + KD):
                    h = u + AHEAD
                    if not (last and h >= 24):
                        ve.wait_ge(hi_done, 24 * e + h + 1)
                        hi, lo = split_half(h)
                        ve.tensor_tensor(lo, stage_half(h), hi, ALU.subtract).then_inc(lo_done, 1)
                    if u < KF:
                        ve.wait_ge(sil_done, 16 * e + u + 1)
                        if u >= 4:
                            ve.wait_ge(hid_done, 16 * e + u - 3)
                        ve.tensor_tensor(hid32[:, u % 4], sil[:, u % 2], ps[:, u % 3, SLOTS:2 * SLOTS], ALU.mult)\
                            .then_inc(prod_done, 1)
                    if u == KF + KD // 2 and not last:
                        modulate_rows(3 * e + 3)
                ve.wait_ge(gated, 5 * e + (2 if last else 4))
                for n, (g, half, bank) in enumerate(((1, 0, 3), (1, 1, 4), (0, 0, 5), (0, 1, 6))):
                    c = (CAP_P, CAP_S)[g]
                    ve.wait_ge(yt_done, 4 * e + n + 1)
                    ve.scalar_tensor_tensor(out=(yeP, yeS)[g][0:c, half * 512:half * 512 + 512], in0=ps[0:c, bank],
                                            scalar=gv[g][:, bass.ds(e, 1)], in1=gt2b[0:c, g, half * 512:half * 512 + 512],
                                            op0=ALU.mult, op1=ALU.mult).then_inc(ye_done, 1)

            with ve.Fori(0, NE - 1) as e:
                expert_vec(e, False)
            expert_vec(NE - 1, True)
            ve.wait_ge(nf_in, 16)
            for t in range(NT):
                ve.wait_ge(f_ss, t + 1)
                ve.tensor_scalar(rs[:, t % 2, 5:6], rs[:, t % 2, 4:5], 1.0 / D, EPS, ALU.mult, ALU.add).then_inc(f_v, 1)
                ve.wait_ge(f_sq, t + 1)
                link(ve.reciprocal(rs[:, t % 2, 7:8], rs[:, t % 2, 6:7]))
                ve.scalar_tensor_tensor(out=finy[:, t], in0=fin[:, t], scalar=rs[:, t % 2, 7:8], in1=nfb,
                                        op0=ALU.mult, op1=ALU.mult).then_inc(y_ready, 1)

        @block.tensor
        def _(pe):
            freed = {}
            uses = [0, 0, 0]
            for n, (s, _) in enumerate(jobs):
                if s[0] == "br":
                    freed[n] = (brow_ready, s[1] + 1)
                elif s[0] == "AR":
                    freed[n] = (modrow_ready, s[1] + 1)
                elif s[0] == "AC":
                    freed[n] = (mod_ready, s[1] + 1)
                elif s[0] == "GT":
                    freed[n] = (gt_ready, s[1] + 1)
                elif s[0] == "I":
                    freed[n] = (idx_ready, jobs[n][1] + 1)
                else:
                    uses[n % 3] += 1
                    freed[n] = (t_free[n % 3], uses[n % 3])

            def bank(s, n=0):
                j = job_at[(s, n)]
                if j >= 3:
                    pe.wait_ge(*freed[j - 3])
                return ps[:, bank_of(j)]

            def split_product(out, w, x, start, stop):
                w_hi, w_lo = w
                x_hi, x_lo = x
                pe.matmul(out, w_hi, x_hi, start=start, stop=False)
                pe.matmul(out, w_hi, x_lo, start=False, stop=False)
                return pe.matmul(out, w_lo, x_hi, start=False, stop=stop)

            def drained():
                for q in range(3):
                    pe.wait_ge(*freed[last_job[0] - q])

            last_job = [0]
            for s in steps:
                k = s[0]
                js = t_jobs(s, items)
                if js:
                    last_job[0] = job_at[js[-1]]
                if k == "vec":
                    pe.wait_ge(small_in, 16 * 7)
                    pe.wait_ge(const, 5)
                    b = bank(s)
                    pe.transpose(b[:, 0:80], vec[:], ident[0:80, 0:80]).then_inc(t_done, 1)
                if k == "br":
                    if s[1] == 0:
                        pe.wait_ge(relb_ready, 1)
                    b = bank(s)
                    pe.matmul(b[:, 0:RELW], relb[:, s[1], :], oneh, start=True, stop=True).then_inc(t_done, 1)
                if k == "AR":
                    c = s[1]
                    b = bank(s)
                    if c == 0:
                        pe.wait_ge(cs_ready, 1)
                    pe.wait_ge(ada_in[c] if c < 4 else ada_in[4 + c % 2], 16 if c < 4 else 16 * (c // 2 - 1))
                    wv = at(ada_slot[c], KD, 512)
                    for kk in range(KD):
                        q = kk % 4
                        ins = pe.matmul(b[32 * q:32 * q + 32, :], cS[:, kk, :], wv[:, kk, :], start=(kk < 4), stop=(kk >= 4),
                                        tile_position=(0, 32 * q))
                    ins.then_inc(t_done, 1)
                if k == "AC":
                    c = s[1]
                    b = bank(s)
                    pe.wait_ge(modrow_ready, c + 1)
                    pe.wait_ge(const, 9)
                    mr = (modrow0 if c < 4 else modrow1)[:, c % 2]
                    for q in range(4):
                        ins = pe.matmul(b[:, 2 * q:2 * q + 2], mr[:, q * P:(q + 1) * P], sel[:], start=(q == 0), stop=True,
                                        skip_group_check=True)
                    ins.then_inc(t_done, 1)
                if k in ("X", "X2"):
                    t = s[1]
                    pe.wait_ge(xn_ready if k == "X" else xn2_ready, t + 1)
                    src = (xn if k == "X" else xn2)[:, t % 2]
                    for half in range(2):
                        b = bank(s, half)
                        for q in range(4):
                            kk = half * 4 + q
                            ins = pe.transpose(b[:, q * P:(q + 1) * P], src[:, kk * P:(kk + 1) * P], ident[:])
                        ins.then_inc(t_done, 1)
                if k == "G":
                    t = s[1]
                    jx = job_at[(("X", t), 1)]
                    pe.wait_ge(*freed[jx])
                    pe.wait_ge(*freed[jx - 1])
                    for c in range(3):
                        n = 3 * t + c
                        if t == 0:
                            pe.wait_ge(win_in, 48)
                        if n >= 5:
                            pe.wait_ge(g_free[n % 5], n // 5)
                        for kk in range(KD):
                            ins = pe.matmul(ps[:, n % 5], hT[:, kk, t * P:(t + 1) * P], wqkv[c][:, kk, :],
                                            start=(kk == 0), stop=(kk == KD - 1))
                        ins.then_inc(g_done, 1)
                if k == "Q":
                    t = s[1]
                    pe.wait_ge(qf_ready, t + 1)
                    f = qf[:, t % 2]
                    b = bank(s, 0)
                    for j in range(NPAIR):
                        ins = pe.transpose(b[:, j * P:(j + 1) * P], f[:, 2 * j:2 * j + 2, :], ident[:])
                    ins.then_inc(t_done, 1)
                    b = bank(s, 1)
                    for j in range(NPAIR):
                        ins = pe.transpose(b[:, j * P:(j + 1) * P], rawB[:, j], ident[:])
                    ins.then_inc(t_done, 1)
                    b = bank(s, 2)
                    pe.transpose(b[:, 0:P], f[:, 8:10, :], ident[:])
                    pe.transpose(b[:, P:2 * P], raw[:, 1280:1408], ident[:]).then_inc(t_done, 1)
                if k == "S":
                    i = s[1]
                    br, j, qt, kts = items[i]
                    k0, w = kts[0] * P, len(kts) * P
                    if i == 0:
                        drained()
                        for n in range(3 * NT - 5, 3 * NT):
                            pe.wait_ge(g_free[n % 5], n // 5 + 1)
                    for hh in range(2):
                        if i >= 1:
                            if items[i - 1][0] == 0:
                                pe.wait_ge(e_done, n_exp(i - 1, hh))
                            else:
                                pe.wait_ge(b_done, n_add(i - 1, hh))
                        for a in range(0, w, 512):
                            z = min(a + 512, w)
                            ins = pe.matmul(ps[:, 2 * hh + a // 512, 0:z - a], qT[:, br, j, qt * P:(qt + 1) * P],
                                            kz[:, br, hh, k0 + a:k0 + z], start=True, stop=True)
                        ins.then_inc(s_done, 1)
                if k == "T":
                    i = s[1]
                    kts = items[i][3]
                    for hh in range(2):
                        pe.wait_ge(pn_vec if by_vec(i, hh) else pn_pool, n_norm(i, hh))
                        for a in range(0, len(kts), 4):
                            n = min(4, len(kts) - a)
                            b = bank(s, (hh, a))
                            for q in range(n):
                                ins = pe.transpose(b[:, q * P:(q + 1) * P], probs(i, hh)[:, (a + q) * P:(a + q + 1) * P],
                                                   ident[:])
                            ins.then_inc(t_done, 1)
                if k == "PV":
                    i = s[1]
                    br, j, qt, kts = items[i]
                    for job in t_jobs(("T", i), items):
                        pe.wait_ge(*freed[job_at[job]])
                    if i >= 1:
                        pe.wait_ge(o_done, i)
                    for n, kt in enumerate(kts):
                        for hh in range(2):
                            ins = pe.matmul(ps[hh * 64:hh * 64 + 64, 4, 0:P], V[:, br, kt, hh * 64:hh * 64 + 64],
                                            PT[:, i % 2, hh, n, :], start=(n == 0), stop=(n == len(kts) - 1),
                                            tile_position=(0, 64 * hh))
                    ins.then_inc(pv_done, 1)
                if k == "GT":
                    b = bank(s)
                    pe.wait_ge(dg_ready, s[1] + 1)
                    for q in range(4):
                        ins = pe.matmul(b[:, q * P:(q + 1) * P], ones[:], dg[:, s[1] % 2, q, :], start=(q == 0), stop=True,
                                        skip_group_check=True)
                    ins.then_inc(t_done, 1)
                if k == "M":
                    m, c = s[1], s[2]
                    n = m * 3 + c
                    w = 256 if c == 2 else 512
                    if n == 0:
                        drained()
                        pe.wait_ge(o_done, NI)
                        pe.wait_ge(e_done, 2 * NI)
                    if c == 0:
                        pe.wait_ge(ws_done, m + 1)
                    if m == 0:
                        pe.wait_ge(hs_done, c + 1)
                    if n >= 2:
                        pe.wait_ge(mm_ready, n - 1)
                    part = [mws[m % 2] + MW // 2 * q for q in range(2)]
                    for b in range(2):
                        wg = [half_words(o + KD * P // 2 * b, KD, P) for o in part]
                        for kk in range(KD):
                            split_product(ps[:, 4 * (n % 2) + b, 0:w], [x[:, kk, :] for x in wg],
                                          [hTs[:, q * KD + kk, c * 512:c * 512 + w] for q in range(2)],
                                          kk == 0, kk == KD - 1)
                    for b in range(2):
                        wb = [half_words(o + KD * P + NPAIR * P // 2 * b, NPAIR, P) for o in part]
                        out = ps[:, 4 * (n % 2) + 2 + b, 0:w].rearrange("p (t q) -> p t q", q=P)
                        for kk in range(NPAIR):
                            ins = split_product(out, [x[:, kk, :] for x in wb],
                                                [oT[:, NPAIR * b + kk, 4 * c:4 * c + w // P, q * P:(q + 1) * P]
                                                 for q in range(2)], kk == 0, kk == NPAIR - 1)
                    ins.then_inc(m_done, 1)
                if k == "O":
                    t = s[1]
                    if t == 0:
                        pe.wait_ge(mm_ready, 3 * KD)
                        pe.wait_ge(merged_ready, 3 * KD)
                    if t >= 2:
                        pe.wait_ge(out_free, t - 1)
                    for h in range(2):
                        pe.wait_ge(wo_in[h], 16)
                        for kk in range(KD):
                            ins = pe.matmul(ps[:, 2 * (t % 2) + h], merged[:, kk, t * P:(t + 1) * P], wo[h][:, kk, :],
                                            start=(kk == 0), stop=(kk == KD - 1))
                    ins.then_inc(out_done, 1)
                if k == "RT":
                    t = s[1]
                    jx = job_at[(("X2", t), 1)]
                    pe.wait_ge(*freed[jx])
                    pe.wait_ge(*freed[jx - 1])
                    if t >= 1:
                        pe.wait_ge(rexp, t)
                    if t == 0:
                        pe.wait_ge(table_in, 16 * 10)
                    for kk in range(KD):
                        ins = pe.matmul(ps[:, 4, 0:NE], h2T[t % 2][:, kk, :], wr[:, kk, :], start=(kk == 0), stop=(kk == KD - 1))
                    ins.then_inc(r_done, 1)
                if k == "AT":
                    t = s[1]
                    pe.wait_ge(aff_ready, t + 1)
                    b = bank(s)
                    pe.transpose(b[0:NE, 0:P], af[:, t % 2], ident[:]).then_inc(t_done, 1)
                if k == "I":
                    pe.wait_ge(topk_ready, 2)
                    for n in range(4):
                        b = bank(s, n)
                        g, what = n // 2, n % 2
                        c = (CAP_P, CAP_S)[g]
                        pe.transpose(b[0:c, 0:NE], (top if what else tif)[g][:], ident[0:NE, 0:NE]).then_inc(t_done, 1)

            def xe_transposes():
                for b3 in range(3):
                    for d in range(3 * b3, min(3 * b3 + 3, KD)):
                        o = (d - 3 * b3) * SLOTS
                        pe.transpose(ps[:, 5 + b3, o:o + CAP_S], xeS[:, d * P:(d + 1) * P], ident[:])
                        ins = pe.transpose(ps[:, 5 + b3, o + CAP_S:o + SLOTS], xeP[:, d * P:(d + 1) * P],
                                           ident[0:CAP_P, 0:CAP_P])
                    ins.then_inc(xe_done, 1)

            pe.wait_ge(idx_ready, 4)
            pe.wait_ge(gat[0], 16)
            pe.wait_ge(gat[1], 16)
            xe_transposes()
            def expert_tensor(e, last):
                pe.wait_ge(xe_ready, 3 * e + 3)
                for f in range(KF):
                    cg, cu = 2 * (f // 4), 2 * (f // 4) + 1
                    if f >= 3:
                        pe.wait_ge(prod_done, 16 * e + f - 2)
                    if f % 4 == 0:
                        pe.wait_ge(lo_done, 24 * e + 2 * cu + 2)
                    cols = slice((f % 4) * P, (f % 4 + 1) * P)
                    for half, c in enumerate((cg, cu)):
                        wv = [half_words(split[c % 6] + n * CH // 2, KD, 512) for n in range(2)]
                        for kk in range(KD):
                            ins = split_product(ps[:, f % 3, half * SLOTS:(half + 1) * SLOTS],
                                                [w[:, kk, cols] for w in wv], [xeT[:, n, kk] for n in range(2)],
                                                kk == 0, kk == KD - 1)
                    ins.then_inc(gu_done, 1)
                pe.wait_ge(hid_done, 16 * e + 16)
                pe.wait_ge(ye_done, 4 * e + 1)
                for d in range(KD):
                    c = 8 + d // 2
                    if d % 2 == 0:
                        pe.wait_ge(lo_done, 24 * e + 2 * c + 2)
                    if d >= 2:
                        pe.wait_ge(yT_done, 8 * e + d - 1)
                    cols = slice((d % 2) * P, (d % 2 + 1) * P)
                    wv = [half_words(split[c % 6] + n * CH // 2, KF, 256) for n in range(2)]
                    for kf in range(KF):
                        ins = split_product(ps[:, 3 + d % 2, 0:SLOTS], [w[:, kf, cols] for w in wv],
                                            [hidT[:, n, kf] for n in range(2)], kf == 0, kf == KF - 1)
                    ins.then_inc(dn_done, 1)
                    if d == KD // 2 - 1 and not last:
                        pe.wait_ge(gat[0], 16 * e + 32)
                        pe.wait_ge(gat[1], 16 * e + 32)
                        xe_transposes()
                pe.wait_ge(yT_done, 8 * e + 8)
                for n, (g, half, bk) in enumerate(((1, 0, 3), (1, 1, 4), (0, 0, 5), (0, 1, 6))):
                    if n == 2 and not last:
                        pe.wait_ge(xe_mod, 3 * e + 6)
                    a, z = ((CAP_S, SLOTS), (0, CAP_S))[g]
                    for q in range(4):
                        ins = pe.transpose(ps[0:z - a, bk, q * P:(q + 1) * P], yeT[:, half * 4 + q, a:z], ident[:])
                    ins.then_inc(yt_done, 1)

            with pe.Fori(0, NE - 1) as e:
                expert_tensor(e, False)
            expert_tensor(NE - 1, True)


_INS = ["x_prompt", "x_sample", "c_prompt", "c_sample", "w_ada", "b_ada", "norm1_g", "w_in", "q_norm_g", "k_norm_g",
        "sink", "w_branch_a", "w_branch_b", "w_out", "norm2_g", "w_router", "w_e_gate", "w_e_up", "w_e_down",
        "rel_bias", "norm_f_g"]


def kernel(**inputs):
    import concourse.bacc as _bacc
    from concourse.bass_utils import run_bass_kernel_spmd as _run

    nc = _bacc.Bacc("TRN2", target_bir_lowering=False, num_devices=1)
    arrays, args = {}, []
    cos, sin = rope_tables()
    for name, a in [(n, inputs[n]) for n in _INS] + [("rope_c", cos), ("rope_s", sin), ("onehot", bucket_onehot())]:
        a = np.ascontiguousarray(a)
        arrays[name] = a
        args.append(nc.dram_tensor(name, a.shape, mybir.dt.from_np(a.dtype), kind="ExternalInput").ap())
    for name, shape in (("y_prompt", (1, SEQ, D)), ("y_sample", (1, DEC, D))):
        args.append(nc.dram_tensor(name, shape, F32, kind="ExternalOutput").ap())
    encoder(nc, *args)
    r = _run(nc, [arrays], core_ids=[0])
    return r.results[0]["y_prompt"], r.results[0]["y_sample"]
```
